# Optimizing a Trainium2 kernel written in Bass

```python
import math
import jax, jax.numpy as jnp
from jax import lax
import numpy as np

D_MODEL = 1024
BATCH = 1
SEQ = 512
DEPTH = 2

N_Q_HEADS = 16
N_KV_HEADS = 2
HEAD_DIM = 64
Q_PER_KV = N_Q_HEADS // N_KV_HEADS
WINDOW = 128
ATTN_BLOCK = 128
ROPE_THETA = 500000.0
ROT_DIM = HEAD_DIM // 4
SGU_WIDTH = 1024
SGU_GROUPS = 8
SGU_GROUP_DIM = SGU_WIDTH // SGU_GROUPS
SGU_CHUNK = 128
FFN_DIM = 2816
CONV_WIDTH = 3
NORM_EPS = 1e-6

Q_END = N_Q_HEADS * HEAD_DIM
K_END = Q_END + N_KV_HEADS * HEAD_DIM
V_END = K_END + N_KV_HEADS * HEAD_DIM
Z_END = V_END + 2 * SGU_WIDTH
IN_COLS = Z_END + 2 * D_MODEL

kernel_name = "hybrid_gmlp_swa_sink_convffn_adaln"

def rms_norm(x, w):
    xf = x.astype(jnp.float32)
    y = xf * lax.rsqrt(jnp.mean(xf * xf, axis=-1, keepdims=True) + NORM_EPS)
    return (y * w.astype(jnp.float32)).astype(x.dtype)

def layer_norm(x, w, b):
    xf = x.astype(jnp.float32)
    mu = jnp.mean(xf, axis=-1, keepdims=True)
    var = jnp.mean(jnp.square(xf - mu), axis=-1, keepdims=True)
    y = (xf - mu) * lax.rsqrt(var + NORM_EPS)
    return (y * w.astype(jnp.float32) + b.astype(jnp.float32)).astype(x.dtype)

def rope_tables(positions, dtype):
    inv_freq = ROPE_THETA ** (-jnp.arange(0, ROT_DIM, 2, dtype=jnp.float32) / ROT_DIM)
    ang = positions.astype(jnp.float32)[..., None] * inv_freq
    return jnp.cos(ang)[:, :, None, :].astype(dtype), jnp.sin(ang)[:, :, None, :].astype(dtype)

def apply_partial_rope(x, cos, sin):
    half = ROT_DIM // 2
    x1, x2, xp = x[..., :half], x[..., half:ROT_DIM], x[..., ROT_DIM:]
    return jnp.concatenate([x1 * cos - x2 * sin, x2 * cos + x1 * sin, xp], axis=-1)

def sliding_window_attention(q, k, v, sinks):
    B, S = q.shape[0], q.shape[1]
    nb = S // ATTN_BLOCK
    qb = q.reshape(B, nb, ATTN_BLOCK, N_KV_HEADS, Q_PER_KV, HEAD_DIM)
    kb = k.reshape(B, nb, ATTN_BLOCK, N_KV_HEADS, HEAD_DIM)
    vb = v.reshape(B, nb, ATTN_BLOCK, N_KV_HEADS, HEAD_DIM)
    pad = ((0, 0), (1, 0), (0, 0), (0, 0), (0, 0))
    k_band = jnp.concatenate([jnp.pad(kb[:, :-1], pad), kb], axis=2)
    v_band = jnp.concatenate([jnp.pad(vb[:, :-1], pad), vb], axis=2)
    scores = jnp.einsum('bnqhgd,bnkhd->bnhgqk', qb, k_band).astype(jnp.float32) * (HEAD_DIM ** -0.5)
    i = jnp.arange(ATTN_BLOCK)[:, None]
    j = jnp.arange(2 * ATTN_BLOCK)[None, :]
    band = (j > i + ATTN_BLOCK - WINDOW) & (j <= i + ATTN_BLOCK)
    exists = (jnp.arange(nb)[:, None, None] > 0) | (j >= ATTN_BLOCK)[None]
    mask = (band[None] & exists)[None, :, None, None]
    scores = jnp.where(mask, scores, -jnp.inf)
    sink = sinks.astype(jnp.float32).reshape(N_KV_HEADS, Q_PER_KV)[None, None, :, :, None, None]
    m = jnp.maximum(jnp.max(scores, axis=-1, keepdims=True), sink)
    p = jnp.exp(scores - m)
    denom = jnp.sum(p, axis=-1, keepdims=True) + jnp.exp(sink - m)
    out = jnp.einsum('bnhgqk,bnkhd->bnqhgd', (p / denom).astype(v.dtype), v_band)
    return out.reshape(B, S, N_Q_HEADS * HEAD_DIM)

def spatial_gating(z, ln_w, ln_b, w_s, b_s):
    B, S = z.shape[0], z.shape[1]
    u, v = jnp.split(z, 2, axis=-1)
    v = layer_norm(v, ln_w, ln_b)
    vb = v.reshape(B, S // SGU_CHUNK, SGU_CHUNK, SGU_GROUPS, SGU_GROUP_DIM)
    causal = jnp.tril(jnp.ones((SGU_CHUNK, SGU_CHUNK), dtype=bool))
    w = jnp.where(causal[None], w_s, jnp.zeros_like(w_s))
    f = jnp.einsum('gts,bnsgc->bntgc', w, vb) + b_s.T[None, None, :, :, None]
    return u * f.reshape(B, S, SGU_WIDTH)

def conv_ffn(h, w_gate, w_up, conv_w, conv_b, w_down):
    a = h @ w_gate
    S = a.shape[1]
    a_pad = jnp.pad(a, ((0, 0), (CONV_WIDTH - 1, 0), (0, 0)))
    a = conv_b + sum(conv_w[k] * a_pad[:, k:k + S] for k in range(CONV_WIDTH))
    return (jax.nn.silu(a) * (h @ w_up)) @ w_down

def setup_inputs(seed: int = 0) -> dict:
    key = jax.random.key(seed)
    ks = jax.random.split(key, 24)
    L, D = DEPTH, D_MODEL
    nrm = lambda k, shape, s: jax.random.normal(k, shape, jnp.float32) * s
    offsets = jax.random.randint(ks[2], (BATCH, 1), 0, 2048, dtype=jnp.int32)
    return {
        "x": nrm(ks[0], (BATCH, SEQ, D), 1.0),
        "c": nrm(ks[1], (BATCH, D), 1.0),
        "positions": offsets + jnp.arange(SEQ, dtype=jnp.int32)[None, :],
        "ada_w": nrm(ks[3], (L, D, 6 * D), D ** -0.5),
        "ada_b": nrm(ks[4], (L, 6 * D), 0.02),
        "norm1_w": 1.0 + nrm(ks[5], (L, D), 0.05),
        "w_in": nrm(ks[6], (L, D, IN_COLS), D ** -0.5),
        "attn_sinks": nrm(ks[7], (L, N_Q_HEADS), 0.5),
        "sgu_ln_w": 1.0 + nrm(ks[8], (L, SGU_WIDTH), 0.05),
        "sgu_ln_b": nrm(ks[9], (L, SGU_WIDTH), 0.02),
        "sgu_w": nrm(ks[10], (L, SGU_GROUPS, SGU_CHUNK, SGU_CHUNK), SGU_CHUNK ** -0.5),
        "sgu_b": 1.0 + nrm(ks[11], (L, SGU_GROUPS, SGU_CHUNK), 0.05),
        "proj_a": nrm(ks[12], (L, SGU_WIDTH, D), SGU_WIDTH ** -0.5),
        "proj_b": nrm(ks[13], (L, N_Q_HEADS * HEAD_DIM, D), (N_Q_HEADS * HEAD_DIM) ** -0.5),
        "w_out": nrm(ks[14], (L, D, D), D ** -0.5),
        "norm2_w": 1.0 + nrm(ks[15], (L, D), 0.05),
        "ffn_w_gate": nrm(ks[16], (L, D, FFN_DIM), D ** -0.5),
        "ffn_w_up": nrm(ks[17], (L, D, FFN_DIM), D ** -0.5),
        "ffn_conv_w": nrm(ks[18], (L, CONV_WIDTH, FFN_DIM), CONV_WIDTH ** -0.5),
        "ffn_conv_b": nrm(ks[19], (L, FFN_DIM), 0.01),
        "ffn_w_down": nrm(ks[20], (L, FFN_DIM, D), FFN_DIM ** -0.5),
        "final_norm_w": 1.0 + nrm(ks[21], (D,), 0.05),
    }

def reference(x, c, positions, ada_w, ada_b, norm1_w, w_in, attn_sinks, sgu_ln_w, sgu_ln_b, sgu_w, sgu_b,
              proj_a, proj_b, w_out, norm2_w, ffn_w_gate, ffn_w_up, ffn_conv_w, ffn_conv_b, ffn_w_down,
              final_norm_w):
    B, S = x.shape[0], x.shape[1]
    cos, sin = rope_tables(positions, x.dtype)
    c_act = jax.nn.silu(c)
    for l in range(DEPTH):
        mod = (c_act @ ada_w[l] + ada_b[l])[:, None, :]
        sh1, sc1, g1, sh2, sc2, g2 = jnp.split(mod, 6, axis=-1)
        h = rms_norm(x, norm1_w[l]) * (1 + sc1) + sh1
        proj = h @ w_in[l]
        q, k, v, z, gates = jnp.split(proj, [Q_END, K_END, V_END, Z_END], axis=-1)
        q = apply_partial_rope(q.reshape(B, S, N_Q_HEADS, HEAD_DIM), cos, sin)
        k = apply_partial_rope(k.reshape(B, S, N_KV_HEADS, HEAD_DIM), cos, sin)
        v = v.reshape(B, S, N_KV_HEADS, HEAD_DIM)
        y_attn = sliding_window_attention(q, k, v, attn_sinks[l])
        y_sgu = spatial_gating(jax.nn.gelu(z, approximate=False), sgu_ln_w[l], sgu_ln_b[l], sgu_w[l], sgu_b[l])
        gate_a, gate_b = jnp.split(jax.nn.sigmoid(gates), 2, axis=-1)
        merged = gate_a * (y_sgu @ proj_a[l]) + gate_b * (y_attn @ proj_b[l])
        x = x + g1 * (merged @ w_out[l])
        h2 = rms_norm(x, norm2_w[l]) * (1 + sc2) + sh2
        x = x + g2 * conv_ffn(h2, ffn_w_gate[l], ffn_w_up[l], ffn_conv_w[l], ffn_conv_b[l], ffn_w_down[l])
    return rms_norm(x, final_norm_w)


_drawn_inputs = setup_inputs


def setup_inputs(seed=0):
    import zlib

    import numpy as np

    out = dict(_drawn_inputs(seed))
    spreads = {}
    factors = {'attn_sinks': 8.0, 'sgu_ln_w': 3.954, 'sgu_ln_b': 8.0, 'sgu_b': 2.833, 'ffn_conv_b': 8.0}
    for name, (base, spread) in spreads.items():
        noise = np.random.default_rng([zlib.crc32(name.encode()), seed]).standard_normal(out[name].shape)
        drawn = base * np.exp(spread * noise) if base else spread * noise
        out[name] = __import__('jax').numpy.asarray(drawn.astype(out[name].dtype))
    for name, factor in factors.items():
        out[name] = (out[name] * factor).astype(out[name].dtype)
    return out
```

```python
import math
from contextlib import ExitStack

import numpy as np

import concourse.bass as bass
from concourse import mybir
from concourse.alu_op_type import AluOpType as ALU

F32 = mybir.dt.float32
F32R = mybir.dt.float32r
I32 = mybir.dt.int32
ACT = mybir.ActivationFunctionType
ds = bass.ds

P = 128
D = 1024
S = 512
DEPTH = 2
HEADS = 16
KV_HEADS = 2
HD = 64
ROT = HD // 4
WINDOW = 128
THETA = 500000.0
SGU = 1024
FFN = 2816
CONV = 3
EPS = 1e-6

DT = D // P
NB = S // P
NQ = DT // 2
FT = FFN // P
BC = 2 * P
Q_END = HEADS * HD
K_END = Q_END + KV_HEADS * HD
V_END = K_END + KV_HEADS * HD
U_END = V_END + SGU
Z_END = U_END + SGU
HALF_Q = Q_END // 2

B_K, B_V = 0, 1
W_INC = 64
B_ZV = 2
B_Q = B_ZV + 4
B_M = B_Q + 16
B_O = B_M + 8
B_F = B_O + 4
B_D = B_F + 2 * (FT // 2)
BLOCKS = B_D + 16
SEGS = [(0, 6), (6, 12), (12, 17), (17, 22)]
NF = FT // 2

U_ZV, U_Q, U_M, U_O, U_F, U_D, USES = 1, 3, 11, 15, 17, 28, 30

N_MOD = 6 * DT
ADA_HALVES = 2 * N_MOD
M_A, M_M, M_F, M_D = 2 * DT, 4 * DT, 5 * DT, 6 * DT
MOD_SUMS = NQ + 3

V_ADAB, V_N1, V_N2, V_LNW, V_LNB, V_EXTRA = 0, 48, 56, 64, 72, 80
VROWS = 88

MAGIC = 1.5 * 2.0 ** 23
TWO_PI = 2.0 * math.pi
TP1 = float(np.float32(6.28125))
TP2 = float(np.float32(np.float32((TWO_PI - TP1) * 2 ** 20).astype(np.int32) / 2.0 ** 20))
TP3 = float(np.float32(TWO_PI - TP1 - TP2))
PI_IN = float(np.nextafter(np.float32(math.pi), np.float32(0)))

NEG = -1.0e30

C_IDENT, C_MASK, C_FREQ, C_SIGN, C_ROT, C_PASS, C_END = 0, 128, 384, 385, 386, 387, 388


def shape_constants():
    c = np.zeros((P, C_END), np.float32)
    c[:, C_IDENT:C_IDENT + P] = np.eye(P, dtype=np.float32)
    i, j = np.arange(P)[:, None], np.arange(2 * P)[None, :]
    band = (j > i + P - WINDOW) & (j <= i + P)
    c[:, C_MASK:C_MASK + 2 * P] = np.where(band, 0.0, NEG)
    inv = (np.float32(THETA) ** (-np.arange(0, ROT, 2, dtype=np.float32) / np.float32(ROT))).astype(np.float32)
    d = np.arange(P) % HD
    c[:, C_FREQ] = np.where(d < ROT, inv[d % (ROT // 2)], 0.0)
    c[:, C_SIGN] = np.where(d < ROT // 2, -1.0, np.where(d < ROT, 1.0, 0.0))
    c[:, C_ROT] = d < ROT
    c[:, C_PASS] = d >= ROT
    return c


class Chain:

    def __init__(self, eng, sem):
        self.eng, self.sem, self.base, self.n = eng, sem, 0, 0

    def link(self, ins):
        ins.then_inc(self.sem, 1)
        self.n += 1
        self.eng.wait_ge(self.sem, self.base + self.n)

    def enter(self, reg, steps):
        held = (self.base, self.n, steps)
        self.base, self.n = self.base + self.n + reg * steps, 0
        return held

    def leave(self, held, times):
        base, n, steps = held
        assert self.n == steps, f"this loop's body has {self.n} steps, not {steps}"
        self.base, self.n = base, n + times * steps


def trunk_kernel(nc, x, c, positions, ada_w, ada_b, norm1_w, w_in, attn_sinks, sgu_ln_w, sgu_ln_b, sgu_w,
                 sgu_b, proj_a, proj_b, w_out, norm2_w, ffn_w_gate, ffn_w_up, ffn_conv_w, ffn_conv_b,
                 ffn_w_down, final_norm_w, consts, out):
    KB = 1024
    start = 192

    def at(name, shape, dtype, offset):
        return nc.alloc_sbuf_tensor_at(name, shape, dtype, offset=offset)

    o = start
    X = at("X", [P, DT, S], F32, o); o += 16 * KB
    HH = at("HH", [P, DT, S], F32R, o)
    HL = at("HL", [P, DT, S], F32R, o + 16 * KB)
    YSH = at("YSH", [P, DT, S], F32R, o)
    YSL = at("YSL", [P, DT, S], F32R, o + 16 * KB)
    OUT_T = at("OUT_T", [P, NB, D], F32, o + 16 * KB)
    o += 32 * KB
    big = o
    FH = at("FH", [P, FT, S], F32R, big)
    FL = at("FL", [P, FT, S], F32R, big + 44 * KB)
    ADA0 = at("ADA0", [P, DT, DT, BC], F32, big)
    YAF = at("YAF", [P, DT, S], F32, big)
    YAL = at("YAL", [P, DT, S], F32R, big)
    YSF = at("YSF", [P, DT, S], F32, big + 16 * KB)
    FIN = [at(f"FIN{n}", [P, 4, S], F32, big + n * 8 * KB) for n in range(2)]
    GA = at("GA", [P, DT, S], F32, big + 32 * KB)
    ML = at("ML", [P, DT, S], F32R, big + 32 * KB)
    GB = at("GB", [P, DT, S], F32, big + 48 * KB)
    MH = at("MH", [P, DT, S], F32R, big + 48 * KB)
    v0 = big + 64 * KB
    ZVF = at("ZVF", [P, DT, S], F32, v0)
    QF = at("QF", [P, 2, S], F32, v0)
    PTH = at("PTH", [P, 2, 2, P], F32R, v0 + 4 * KB)
    PTL = at("PTL", [P, 2, 2, P], F32R, v0 + 6 * KB)
    WRAW = at("WRAW", [P, 2, P], F32, v0 + 8 * KB)
    WT = at("WT", [P, 2, P], F32, v0 + 9 * KB)
    RB = at("RB", [P, 2, P], F32, v0 + 10 * KB)
    SM = [at(f"SM{n}", [P, 2, 2 * P + 1], F32, v0 + 11 * KB + n * 2080) for n in range(2)]
    ADA_ACCM = at("ADA_ACCM", [P, DT, P], F32, v0)
    k0 = v0 + 16 * KB
    KP = at("KP", [P, KV_HEADS, S], F32, k0)
    VH = at("VH", [P, NB, P], F32R, k0 + 4 * KB)
    VL = at("VL", [P, NB, P], F32R, k0 + 6 * KB)
    o += 88 * KB
    e0 = o
    XT = at("XT", [P, NB, D], F32, e0)
    VT = at("VT", [P, NB, D], F32, e0)
    YAH = at("YAH", [P, DT, S], F32R, e0)
    CONVT = at("CONVT", [P, 2, S], F32, e0)
    ADA_ACCF = at("ADA_ACCF", [P, DT, P], F32, e0 + 4 * KB)
    ADA_ACCD = at("ADA_ACCD", [P, 2 * DT, P], F32, e0 + 8 * KB)
    o += 16 * KB
    WS = at("WS", [P, 2, DT, BC], F32, o); o += 16 * KB
    WH = at("WH", [P, 2, DT, BC], F32R, o); o += 16 * KB
    WL = at("WL", [P, 2, DT, BC], F32R, o); o += 16 * KB
    t0 = o
    VN = at("VN", [P, NB, BC], F32, t0)
    ADA_ACCA = at("ADA_ACCA", [P, 4, P], F32, t0 + 6 * KB)
    VRAW = at("VRAW", [P, S], F32, t0)
    SQ0 = [at(f"SQ0{n}", [P, S], F32, k0 + n * 2 * KB) for n in range(2)]
    RS = at("RS", [P, S], F32, t0)
    VR = at("VR", [VROWS, 4, P], F32, t0)
    T1 = at("T1", [P, S], F32, t0 + 2 * KB)
    T2 = at("T2", [P, S], F32, t0 + 4 * KB)
    T3 = at("T3", [P, S], F32, t0 + 6 * KB)
    POS = at("POS", [P, S], I32, t0 + 2 * KB)
    ROTT = T2
    ACC = at("ACC", [P, S], F32, t0 + 4 * KB)
    SQ = [T1, T3]
    NT = [T1, T3]
    o += 8 * KB
    ADA = at("ADA", [P, 2, 4, P], F32, o); o += 4 * KB
    COS = at("COS", [P, S], F32, o); o += 2 * KB
    SIN = at("SIN", [P, S], F32, o); o += 2 * KB
    CST = at("CST", [P, C_END], F32, o); o += 1568
    ONES = at("ONES", [P, P], F32, o); o += 512
    VEC = at("VEC", [P, DEPTH, 2, VROWS], F32, o); o += 1408
    MOD = at("MOD", [P, DEPTH, N_MOD], F32, o); o += 384
    SINK = at("SINK", [P, DEPTH, KV_HEADS, HEADS // 2], F32, o); o += 128
    SINKC = at("SINKC", [P, KV_HEADS, 2], F32, o); o += 32
    CACT = at("CACT", [P, DT], F32, o); o += 32
    WSC = at("WSC", [P, DT], F32, o); o += 32
    SHC = at("SHC", [P, DT], F32, o); o += 32
    MX = at("MX", [P, 2, 2], F32, o); o += 32
    NM = at("NM", [P, 2, 2], F32, o); o += 32
    DEN = at("DEN", [P, 2, 2], F32, o); o += 32
    RDEN = at("RDEN", [P, 2, 2], F32, o); o += 32
    BN = at("BN", [P, NB, 12], F32, o); o += 192
    MV = at("MV", [P, NB, 2], F32, o); o += 32
    SD = at("SD", [P, NB], F32, o); o += 32
    RSV = at("RSV", [P, NB], F32, o); o += 32
    EPSC = at("EPSC", [P, 1], F32, o); o += 32
    assert o <= nc.sbuf_usable_end, (o, nc.sbuf_usable_end)
    IDENT = CST[:, C_IDENT:C_IDENT + P]

    w_in_v = w_in.rearrange("l (k p) n -> p l k n", p=P)
    proj_a_v = proj_a.rearrange("l (k p) n -> p l k n", p=P)
    proj_b_v = proj_b.rearrange("l (s k p) n -> s p l k n", s=KV_HEADS, p=HD)
    w_out_v = w_out.rearrange("l (k p) n -> p l k n", p=P)
    gate_v = ffn_w_gate.rearrange("l (k p) n -> p l k n", p=P)
    up_v = ffn_w_up.rearrange("l (k p) n -> p l k n", p=P)
    down_v = ffn_w_down.rearrange("l (k p) n -> p l k n", p=P)
    ada_v = ada_w.rearrange("l (k p) n -> p l k n", p=P)
    sgu_w_v = sgu_w.rearrange("l g t s -> t l g s")

    with ExitStack() as ctx:
        def sem(name):
            return ctx.enter_context(nc.semaphore(name))

        PS = ctx.enter_context(nc.psum_tensor("PS", [P, 8, S], F32))

        w_loaded = [sem("w_loaded0"), sem("w_loaded1")]
        w_hi = sem("w_hi")
        w_lo = sem("w_lo")
        blk_done = sem("blk_done")
        bank_free = [sem("bank_free0"), sem("bank_free1")]
        sq_ready = sem("sq_ready")
        x_ready = sem("x_ready")
        acc_zero = sem("acc_zero")
        sq_added = sem("sq_added")
        stat_ready = sem("stat_ready")
        rms_root = sem("rms_root")
        h_pre = sem("h_pre")
        h_hi = sem("h_hi")
        h_lo = sem("h_lo")
        rope_cos = sem("rope_cos")
        rope_out = sem("rope_out")
        v_trans = sem("v_trans")
        v_hi = sem("v_hi")
        v_lo = sem("v_lo")
        zt_trans = sem("zt_trans")
        zt_copied = sem("zt_copied")
        ln_var = sem("ln_var")
        ln_root = sem("ln_root")
        ln_ready = sem("ln_ready")
        mixw_loaded = sem("mixw_loaded")
        mixb_loaded = sem("mixb_loaded")
        mixw_causal = sem("mixw_causal")
        mixw_trans = sem("mixw_trans")
        mixw_ready = sem("mixw_ready")
        rowsum_ready = sem("rowsum_ready")
        mixb_ready = sem("mixb_ready")
        vn_ready = sem("vn_ready")
        mixed = sem("mixed")
        u_ready = sem("u_ready")
        y_raw = sem("y_raw")
        y_hi = sem("y_hi")
        y_lo = sem("y_lo")
        s_ready = sem("s_ready")
        s_used = sem("s_used")
        nm_ready = sem("nm_ready")
        p_ready = sem("p_ready")
        rden_ready = sem("rden_ready")
        pn_ready = sem("pn_ready")
        pt_ready = sem("pt_ready")
        pt_hi = sem("pt_hi")
        pt_lo = sem("pt_lo")
        o_ready = sem("o_ready")
        ya_out = sem("ya_out")
        m_sum = sem("m_sum")
        m_hi = sem("m_hi")
        m_lo = sem("m_lo")
        ada_loaded = [sem(f"ada_loaded{n}") for n in range(2)]
        ada_used = sem("ada_used")
        ada_cols = sem("ada_cols")
        mod_ready = sem("mod_ready")
        conv_pre = sem("conv_pre")
        silu_done = sem("silu_done")
        f_hi = sem("f_hi")
        f_lo = sem("f_lo")
        waits_passed = sem("waits_passed")
        act_chain = sem("act_chain")
        dve_chain = sem("dve_chain")
        pool_chain = sem("pool_chain")
        const_in = sem("const_in")
        x_in = sem("x_in")
        rows_in = sem("rows_in")
        sinks_in = sem("sinks_in")
        pos_in = sem("pos_in")
        ada0_in = [sem(f"ada0_in{n}") for n in range(DT)]
        ones_set = sem("ones_set")
        vec_trans = sem("vec_trans")
        vec_ready = sem("vec_ready")
        x_trans = sem("x_trans")
        cact_ready = sem("cact_ready")
        angle_ready = sem("angle_ready")
        sine_ready = sem("sine_ready")
        fin_tile = sem("fin_tile")
        out_trans = sem("out_trans")
        out_copied = sem("out_copied")
        out_stored = sem("out_stored")

        block = ctx.enter_context(nc.Block())

        def alone(eng):
            eng.sem_inc(waits_passed, 1)

        def bank_pair(s):
            return PS[:, 2 * s:2 * s + 2, :]

        @block.sync
        def _(sp):
            sp.dma_start(CST[:], consts).then_inc(const_in, 16)
            row = 0
            for l in range(DEPTH):
                for src, r0, n in ((ada_b, V_ADAB, 48), (norm1_w, V_N1, 8), (norm2_w, V_N2, 8),
                                   (sgu_ln_w, V_LNW, 8), (sgu_ln_b, V_LNB, 8)):
                    sp.dma_start(VR[r0:r0 + n, 2 * l, :], src[l].rearrange("(r p) -> r p", p=P)).then_inc(rows_in, 16)
                sp.dma_start(VR[0:CONV * FT, 2 * l + 1, :],
                             ffn_conv_w[l].rearrange("t (r p) -> (t r) p", p=P)).then_inc(rows_in, 16)
                sp.dma_start(VR[CONV * FT:VROWS, 2 * l + 1, :],
                             ffn_conv_b[l].rearrange("(r p) -> r p", p=P)).then_inc(rows_in, 16)
            sp.dma_start(VR[V_EXTRA:VROWS, 0, :], final_norm_w.rearrange("(r p) -> r p", p=P)).then_inc(rows_in, 16)
            sp.dma_start(VR[V_EXTRA:VROWS, 2, :], c[0].rearrange("(r p) -> r p", p=P)).then_inc(rows_in, 16)
            sp.dma_start(XT[:], x[0].rearrange("(b p) d -> p b d", p=P)).then_inc(x_in, 16)
            for n in range(DT):
                sp.dma_start(ADA0[:, n], ada_v[:, 0, :, n * BC:(n + 1) * BC]).then_inc(ada0_in[n], 16)
            sp.dma_start(POS[:], positions.to_broadcast([P, S])).then_inc(pos_in, 16)
            sp.dma_start(SINK[:], attn_sinks.rearrange("l h -> (l h)")[None, :].to_broadcast([P, DEPTH * HEADS])
                         .rearrange("p (l s h) -> p l s h", l=DEPTH, s=KV_HEADS)).then_inc(sinks_in, 16)

            with sp.Fori(0, DEPTH) as l:
                def load(n, slot, parts):
                    sp.wait_ge(w_lo, BLOCKS * l + n + 1)
                    for dst, src in parts:
                        sp.dma_start(dst, src).then_inc(w_loaded[slot], W_INC // len(parts))

                def load_block(n, slot, view, c0, k0=0, k1=DT, width=BC):
                    load(n, slot, [(WS[:, slot:slot + 1, 0:k1 - k0, 0:width],
                                    view[:, ds(l, 1), k0:k1, ds(c0, width)])])

                load_block(B_K, 0, w_in_v, Q_END, width=P)
                load_block(B_V, 1, w_in_v, K_END, width=P)
                with sp.Fori(0, 2) as i:
                    for s in range(2):
                        load_block(B_ZV + i * 2 + s, s, w_in_v, U_END + (i * 2 + s) * BC)
                with sp.Fori(0, NQ) as i:
                    load(B_Q + i * 4, 0, [(WS[:, 0:1, :, (2 * t + h) * HD:(2 * t + h + 1) * HD],
                                           w_in_v[:, ds(l, 1), :, ds(h * HALF_Q + t * HD + i * P, HD)])
                                          for t in range(2) for h in range(KV_HEADS)])
                    load_block(B_Q + i * 4 + 1, 1, w_in_v, V_END + i * BC)
                    sp.wait_ge(zt_trans, NB * l + NB)
                    sp.wait_ge(mixw_trans, NQ * l + i + 1)
                    sp.dma_start(WRAW[:, None], sgu_w_v[:, ds(l, 1), ds(2 * i, 2), :]).then_inc(mixw_loaded, 16)
                    sp.wait_ge(y_raw, 2 * (NQ * l + i) + 1)
                    sp.dma_start(RB[:], sgu_b[ds(l, 1), ds(2 * i, 2), :].to_broadcast([P, 2, P])).then_inc(mixb_loaded, 16)
                    load_block(B_Q + i * 4 + 2, 0, w_in_v, Z_END + i * BC)
                    load_block(B_Q + i * 4 + 3, 1, w_in_v, Z_END + D + i * BC)
                with sp.Fori(0, NQ) as j:
                    load_block(B_M + j * 2, 0, proj_a_v, j * BC)
                    load(B_M + j * 2 + 1, 1, [(WS[h * HD:(h + 1) * HD, 1:2, :, :],
                                               proj_b_v[h][:, ds(l, 1), :, ds(j * BC, BC)]) for h in range(KV_HEADS)])
                with sp.Fori(0, 2) as i:
                    for s in range(2):
                        load_block(B_O + i * 2 + s, s, w_out_v, (i * 2 + s) * BC)
                with sp.Fori(0, NF) as j:
                    load_block(B_F + j * 2, 0, gate_v, j * BC)
                    load_block(B_F + j * 2 + 1, 1, up_v, j * BC)
                with sp.Fori(0, NQ) as g:
                    for n, (k0, k1) in enumerate(SEGS):
                        load_block(B_D + g * 4 + n, n % 2, down_v, g * BC, k0, k1)

            outv = out[0].rearrange("(b p) d -> p b d", p=P)
            for half in range(2):
                sp.wait_ge(out_copied, 4 * (half + 1))
                sp.dma_start(outv[:, :, half * S:(half + 1) * S],
                             OUT_T[:, :, half * S:(half + 1) * S]).then_inc(out_stored, 16)
            sp.wait_ge(out_stored, 32)

        @block.tensor
        def _(pe):
            pe.sem_inc(blk_done, 2)
            pe.sem_inc(mixw_trans, 1)

            def products(out_ap, slot, cols, xh, xl, kw, kx, first, last):
                wh, wl = WH[:, slot, kw, cols], WL[:, slot, kw, cols]
                nc.tensor.matmul(out_ap, wh, xh[:, kx, :], start=first, stop=False)
                nc.tensor.matmul(out_ap, wh, xl[:, kx, :], start=False, stop=False)
                return nc.tensor.matmul(out_ap, wl, xh[:, kx, :], start=False, stop=last)

            def half(j):
                return slice(j * P, (j + 1) * P)

            def block_ready(n, slot, use, l):
                pe.wait_ge(w_lo, BLOCKS * l + n + 3)
                pe.wait_ge(bank_free[slot], USES * l + use + 1)

            def weight_block(slot, xh, xl, after=None):
                for k in range(DT):
                    for j in range(2):
                        ins = products(PS[:, 2 * slot + j, :], slot, half(j), xh, xl, k, k, k == 0, k == DT - 1)
                    if k == DT - 1:
                        ins.then_inc(blk_done, 1)
                    if after:
                        after(k)

            def columns(bank, col, sums, n, times):
                pe.wait_ge(mod_ready, times)
                for a in range(n):
                    ins = nc.tensor.matmul(PS[:, bank, col + a:col + a + 1], sums[:, a, :], ONES[:, 0:1],
                                           start=True, stop=True)
                ins.then_inc(ada_cols, 1)

            def statistics(nn):
                pe.wait_ge(sq_added, DT * (nn + 1))
                nc.tensor.matmul(PS[:, 4, :], ONES[:], ACC[:], start=True, stop=True).then_inc(stat_ready, 1)

            pe.wait_ge(const_in, 16)
            pe.wait_ge(rows_in, 16 * (7 * DEPTH + 2))
            pe.wait_ge(ones_set, 2)
            for n in range(4):
                ins = nc.tensor.transpose(PS[:, 5, n * VROWS:(n + 1) * VROWS], VR[:, n, :], IDENT[0:VROWS, 0:VROWS])
            ins.then_inc(vec_trans, 1)
            pe.wait_ge(x_in, 16)
            for k in range(DT):
                if k >= 4:
                    pe.wait_ge(x_ready, k - 3)
                for b in range(NB):
                    ins = nc.tensor.transpose(PS[:, k % 4, b * P:(b + 1) * P], XT[:, b, k * P:(k + 1) * P], IDENT)
                ins.then_inc(x_trans, 1)
            pe.wait_ge(cact_ready, 1)
            for m in range(2 * DT):
                if m % 2 == 0:
                    pe.wait_ge(ada0_in[m // 2], 16)
                for k in range(DT):
                    ins = nc.tensor.matmul(PS[:, 7, m:m + 1], ADA0[:, m // 2, k, half(m % 2)], CACT[:, k:k + 1],
                                           start=k == 0, stop=k == DT - 1)
            ins.then_inc(ada_cols, 1)
            pe.wait_ge(x_ready, DT)
            pe.wait_ge(vec_ready, 1)

            with pe.Fori(0, DEPTH) as l:
                statistics(2 * l)
                block_ready(B_K, 0, 0, l)
                block_ready(B_V, 1, 0, l)
                for k in range(DT):
                    pe.wait_ge(h_lo, 2 * DT * l + k + 1)
                    for s in range(2):
                        ins = products(PS[:, 2 * s, :], s, half(0), HH, HL, k, k, k == 0, k == DT - 1)
                        if k == DT - 1:
                            ins.then_inc(blk_done, 1)
                with pe.Fori(0, 2) as i:
                    for s in range(2):
                        block_ready(B_ZV + i * 2 + s, s, U_ZV + i, l)
                        weight_block(s, HH, HL)
                for b in range(NB):
                    ins = nc.tensor.transpose(PS[:, 4, b * P:(b + 1) * P], VRAW[:, b * P:(b + 1) * P], IDENT)
                ins.then_inc(v_trans, 1)
                pe.wait_ge(bank_free[0], USES * l + U_Q + 1)
                pe.wait_ge(bank_free[1], USES * l + U_Q + 1)
                for b in range(NB):
                    lo = 4 + 2 * (b % 2)
                    if b == 0:
                        pe.wait_ge(v_lo, l + 1)
                    if b >= 2:
                        pe.wait_ge(zt_copied, NB * l + b - 1)
                    for t in range(DT):
                        ins = nc.tensor.transpose(PS[:, lo + t // 4, (t % 4) * P:(t % 4 + 1) * P],
                                                  ZVF[:, t, b * P:(b + 1) * P], IDENT)
                    ins.then_inc(zt_trans, 1)
                pe.wait_ge(zt_copied, NB * l + NB)
                alone(pe)

                with pe.Fori(0, NQ) as i:
                    block_ready(B_Q + i * 4, 0, U_Q + i * 2, l)
                    weight_block(0, HH, HL)
                    units = NB * DT * l + NB * 2 * i

                    def scores(u):
                        t, b = u // NB, u % NB
                        if u == 0 or u == NB:
                            pe.wait_ge(rope_out, (DT + 1) * l + 2 * i + t + 2)
                        if u < 2:
                            pe.wait_ge(y_raw, 2 * (NQ * l + i) + 1)
                        else:
                            pe.wait_ge(s_used, units + u - 1)
                        keys = slice(max(0, b - 1) * P, (b + 1) * P)
                        width = keys.stop - keys.start
                        dst = PS[:, 4 + u % 2, :].rearrange("p (h k) -> p h k", h=2)[:, :, 0:width]
                        ins = nc.tensor.matmul(dst, QF[:, t, b * P:(b + 1) * P], KP[:, :, keys], start=True, stop=True)
                        ins.then_inc(s_ready, 1)

                    def transposes(u):
                        b = u % NB
                        pe.wait_ge(pn_ready, units + u + 1)
                        if u == 0:
                            pe.wait_ge(mixb_ready, NQ * l + i + 1)
                        else:
                            pe.wait_ge(pt_lo, units + u)
                        for kb in range(0 if b else 1, 2):
                            for h in range(KV_HEADS):
                                ins = nc.tensor.transpose(PS[:, 6, (2 * kb + h) * P:(2 * kb + h + 1) * P],
                                                          SM[u % 2][:, h, kb * P:(kb + 1) * P], IDENT)
                        ins.then_inc(pt_ready, 1)

                    def outputs(u):
                        b = u % NB
                        pe.wait_ge(pt_lo, units + u + 1)
                        if u % 2 == 0:
                            pe.wait_ge(ya_out, 2 * DT * l + 4 * i + u // 2 + 1)
                        if u == 0:
                            pe.wait_ge(v_lo, l + 1)
                        dst = PS[:, 7, (u % 2) * 2 * P:(u % 2 + 1) * 2 * P]
                        kbs = range(0 if b else 1, 2)
                        for kb in kbs:
                            vb = b - 1 + kb
                            for a, (vv, pp) in enumerate(((VH, PTH), (VH, PTL), (VL, PTH))):
                                ins = nc.tensor.matmul(dst, vv[:, vb, :], pp[:, kb].rearrange("p h q -> p (h q)"),
                                                       start=u % 2 == 0 and kb == kbs[0] and a == 0,
                                                       stop=kb == 1 and a == 2, skip_group_check=True)
                        ins.then_inc(o_ready, 1)

                    def mix(g):
                        pe.wait_ge(s_used, units + 7 + g)
                        if g == 0:
                            pe.wait_ge(vn_ready, NQ * l + i + 1)
                        for b in range(NB):
                            ins = nc.tensor.matmul(PS[:, 4 + g, b * P:(b + 1) * P], VN[:, b, g * P:(g + 1) * P],
                                                   WT[:, g, :], start=b == 0, stop=True, skip_group_check=True)
                        ins.then_inc(mixed, 1)

                    def mix_weights():
                        pe.wait_ge(mixw_causal, NQ * l + i + 1)
                        pe.wait_ge(mod_ready, MOD_SUMS * l + i + 1)
                        for g in range(2):
                            ins = nc.tensor.transpose(PS[:, 6, g * P:(g + 1) * P], WRAW[:, g, :], IDENT)
                        ins.then_inc(mixw_trans, 1)

                    def mix_sums():
                        pe.wait_ge(mixw_ready, NQ * l + i + 1)
                        nc.tensor.matmul(PS[:, 6, 0:2 * P], ONES[:], WT[:].rearrange("p g t -> p (g t)"),
                                         start=True, stop=True).then_inc(rowsum_ready, 1)

                    def attention_step(w):
                        if w < 8:
                            scores(w)
                        if 0 <= w - 3 < 8:
                            outputs(w - 3)
                        if 0 <= w - 2 < 8:
                            transposes(w - 2)
                        if w >= 9:
                            mix(w - 9)
                        if w == 10:
                            pe.wait_ge(ada_used, ADA_HALVES * l + 8 * i + 8 + 2)
                            columns(6, 0, ADA_ACCA, 4, MOD_SUMS * l + i + 1)

                    def between(k):
                        if k == 2:
                            mix_weights()
                        if k == 4:
                            mix_sums()
                        if k >= 3 and k % 2:
                            attention_step((k - 3) // 2)

                    block_ready(B_Q + i * 4 + 1, 1, U_Q + i * 2, l)
                    weight_block(1, HH, HL, between)
                    block_ready(B_Q + i * 4 + 2, 0, U_Q + i * 2 + 1, l)
                    weight_block(0, HH, HL, lambda k: between(DT + k))
                    block_ready(B_Q + i * 4 + 3, 1, U_Q + i * 2 + 1, l)
                    weight_block(1, HH, HL, lambda k: between(2 * DT + k))

                def merge_iteration(j, before):
                    block_ready(B_M + j * 2, 0, U_M + j, l)
                    before(0)
                    weight_block(0, YSH, YSL, lambda k: before(k + 1) if k + 1 < DT else None)
                    block_ready(B_M + j * 2 + 1, 1, U_M + j, l)
                    before(DT)
                    weight_block(1, YAH, YAL, lambda k: before(DT + k + 1) if k + 1 < DT else None)

                merge_iteration(0, lambda tile: pe.wait_ge(y_lo, 2 * DT * l + tile + 1))
                with pe.Fori(1, NQ) as j:
                    merge_iteration(j, lambda tile: None)

                pe.wait_ge(ada_used, ADA_HALVES * l + 2 * (M_F - M_A) + 2)
                columns(7, 0, ADA_ACCM, DT, MOD_SUMS * l + NQ + 1)
                pe.wait_ge(m_lo, NQ * l + NQ)
                alone(pe)
                with pe.Fori(0, 2) as i:
                    for s in range(2):
                        block_ready(B_O + i * 2 + s, s, U_O + i, l)
                        weight_block(s, MH, ML)

                statistics(2 * l + 1)
                block_ready(B_F, 0, U_F, l)

                def ffn_iteration(j, normed):
                    if normed is None:
                        block_ready(B_F + j * 2, 0, U_F + j, l)
                    weight_block(0, HH, HL, normed)
                    block_ready(B_F + j * 2 + 1, 1, U_F + j, l)
                    weight_block(1, HH, HL)

                def follow(a):
                    if a + 1 < DT:
                        pe.wait_ge(h_lo, 2 * DT * l + DT + a + 2)

                pe.wait_ge(h_lo, 2 * DT * l + DT + 1)
                ffn_iteration(0, follow)
                with pe.Fori(1, NF) as j:
                    ffn_iteration(j, None)
                pe.wait_ge(ada_used, ADA_HALVES * l + 2 * (M_D - M_A) + 2)
                columns(7, 0, ADA_ACCF, DT, MOD_SUMS * l + NQ + 2)

                with pe.Fori(0, 2) as i:
                    for s in range(2):
                        for n, (k0, k1) in enumerate(SEGS):
                            pe.wait_ge(w_lo, BLOCKS * l + B_D + i * 8 + s * 4 + n + 3)
                            if n == 0:
                                pe.wait_ge(bank_free[s], USES * l + U_D + i + 1)
                                pe.wait_ge(f_lo, NF * l + NF + 1)
                            for a in range(k1 - k0):
                                for j in range(2):
                                    ins = products(PS[:, 2 * s + j, :], n % 2, half(j), FH, FL, a, k0 + a,
                                                   n == 0 and a == 0, n == 3 and a == k1 - k0 - 1)
                            ins.then_inc(blk_done, 1)

                pe.wait_ge(ada_used, ADA_HALVES * (l + 1) + 2)
                columns(7, 0, ADA_ACCD, 2 * DT, MOD_SUMS * l + NQ + 3)

            statistics(2 * DEPTH)
            for k in range(DT):
                pe.wait_ge(fin_tile, k + 1)
                if k >= 4:
                    pe.wait_ge(out_copied, k - 3)
                for b in range(NB):
                    ins = nc.tensor.transpose(PS[:, k % 4, b * P:(b + 1) * P],
                                              FIN[k % 2][:, k // 2, b * P:(b + 1) * P], IDENT)
                ins.then_inc(out_trans, 1)

        @block.scalar
        def _(act):
            act.sem_inc(w_hi, 2)
            act.sem_inc(ya_out, 1)
            chain = Chain(act, act_chain)
            A = nc.scalar.activation

            def hi(n0, slot, l, i=0, per=0, kts=DT, width=BC):
                act.wait_ge(w_loaded[slot], W_INC * ((BLOCKS // 2) * l + n0 // 2 + i * (per // 2) + 1))
                act.wait_ge(blk_done, BLOCKS * l + n0 + i * per + 1)
                A(WH[:, slot, 0:kts, 0:width], WS[:, slot, 0:kts, 0:width], ACT.Copy).then_inc(w_hi, 1)

            def ada_load(l, n0, number, layer, unit):
                half = number % 2
                act.wait_ge(ada_used, ADA_HALVES * l + n0 + number + 1)
                act.dma_start(ADA[:, half:half + 1], ada_v[:, ds(layer, 1), 4 * half:4 * half + 4, ds(unit * P, P)]
                              ).then_inc(ada_loaded[half], 16)

            def norm_tiles(nn):
                act.wait_ge(stat_ready, nn + 1)
                A(RS[:], PS[:, 4, :], ACT.Sqrt, bias=EPSC[:, 0:1], scale=1.0 / D).then_inc(rms_root, 1)

            def shifted(nn):
                for k in range(DT):
                    act.wait_ge(h_pre, DT * nn + k + 1)
                    A(HH[:, k, :], NT[k % 2][:], ACT.Identity, bias=SHC[:, k:k + 1]).then_inc(h_hi, 1)

            act.wait_ge(ones_set, 2)
            act.wait_ge(vec_trans, 1)
            A(VEC[:].rearrange("p l t r -> p (l t r)"), PS[:, 5, 0:4 * VROWS], ACT.Copy).then_inc(vec_ready, 1)
            act.wait_ge(vec_ready, 1)
            A(CACT[:], VEC[:, 1, 0, V_EXTRA:V_EXTRA + DT], ACT.Silu).then_inc(cact_ready, 1)
            for k in range(DT):
                act.wait_ge(x_trans, k + 1)
                A(X[:, k, :], PS[:, k % 4, :], ACT.Copy).then_inc(x_ready, 1)
                act.wait_ge(x_ready, k + 1)
                if k >= 2:
                    act.wait_ge(sq_added, k - 1)
                A(SQ0[k % 2][:], X[:, k, :], ACT.Square).then_inc(sq_ready, 1)
            act.wait_ge(angle_ready, 1)
            A(SIN[:], SIN[:], ACT.Sin).then_inc(sine_ready, 1)
            A(COS[:], COS[:], ACT.Sin).then_inc(sine_ready, 1)

            with act.Fori(0, DEPTH) as l:
                hi(B_K, 0, l, width=P)
                hi(B_V, 1, l, width=P)
                norm_tiles(2 * l)
                shifted(2 * l)
                ada_load(l, 0, 0, l, M_A)
                act.wait_ge(blk_done, BLOCKS * l + B_V + 3)
                A(VRAW[:], PS[:, 2, :], ACT.Copy).then_inc(bank_free[1], 1)
                hi(B_ZV, 0, l)
                hi(B_ZV + 1, 1, l)
                with act.Fori(0, 2) as i:
                    for s in range(2):
                        act.wait_ge(blk_done, BLOCKS * l + B_ZV + i * 2 + s + 3)
                        alone(act)
                        A(ZVF[:, ds(i * 4 + 2 * s, 2), :], bank_pair(s), ACT.Gelu).then_inc(bank_free[s], 1)
                        hi(B_ZV + 2 + s, s, l, i, 2)
                act.wait_ge(v_trans, l + 1)
                A(VH[:].rearrange("p b d -> p (b d)"), PS[:, 4, :], ACT.Copy).then_inc(v_hi, 1)
                for b in range(NB):
                    act.wait_ge(zt_trans, NB * l + b + 1)
                    lo = 4 + 2 * (b % 2)
                    A(VT[:, b, :], PS[:, lo:lo + 2, :].rearrange("p a n -> p (a n)"), ACT.Copy).then_inc(zt_copied, 1)
                act.wait_ge(ln_var, l + 1)
                A(SD[:], MV[:, :, 1], ACT.Sqrt, bias=EPSC[:, 0:1]).then_inc(ln_root, 1)

                with act.Fori(0, NQ) as i:
                    hi(B_Q + 2, 0, l, i, 4)
                    units = NB * DT * l + NB * 2 * i

                    def exponentials(u):
                        b = u % NB
                        first = 0 if b else P
                        act.wait_ge(nm_ready, units + u + 1)
                        for h in range(KV_HEADS):
                            cols = SM[u % 2][:, h, first:2 * P + 1]
                            ins = A(cols, cols, ACT.Exp, bias=NM[:, u % 2, h:h + 1], accum_out=DEN[:, u % 2, h:h + 1])
                        ins.then_inc(p_ready, 1)

                    def prob_hi(u):
                        first = 0 if u % NB else 1
                        act.wait_ge(pt_ready, units + u + 1)
                        A(PTH[:, first:2].rearrange("p k h q -> p (k h q)"), PS[:, 6, first * 2 * P:],
                          ACT.Copy).then_inc(pt_hi, 1)

                    def attn_out(u):
                        act.wait_ge(o_ready, units + u + 1)
                        alone(act)
                        t, b = u // NB, u % NB - 1
                        src = PS[:, 7, :].rearrange("p (a h q) -> p a h q", a=2, h=2)
                        for h in range(KV_HEADS):
                            rows = slice(h * HD, (h + 1) * HD)
                            dst = YAF[rows, ds(2 * i + t, 1), b * P:(b + 2) * P].rearrange("p o (a q) -> p (o a) q", a=2)
                            ins = A(dst, src[rows, :, h, :], ACT.Copy)
                        ins.then_inc(ya_out, 1)

                    def evacuate(step, dst, func):
                        act.wait_ge(blk_done, BLOCKS * l + B_Q + i * 4 + step + 3)
                        alone(act)
                        A(dst[:, ds(2 * i, 2), :], bank_pair(step % 2), func).then_inc(bank_free[step % 2], 1)

                    for w in range(11):
                        if w < 8:
                            exponentials(w)
                        if 0 <= w - 2 < 8:
                            prob_hi(w - 2)
                        if w - 3 >= 0 and (w - 3) % 2:
                            attn_out(w - 3)
                        if w < 8:
                            ada_load(l, 8 * i, w + 1, l, M_A + 4 * i + (w + 1) // 2)
                        if w == 3:
                            evacuate(1, YSF, ACT.Gelu)
                            hi(B_Q + 3, 1, l, i, 4)
                        if w == 7:
                            evacuate(2, GA, ACT.Sigmoid)
                            hi(B_Q + 4, 0, l, i, 4)
                    evacuate(3, GB, ACT.Sigmoid)
                    hi(B_Q + 5, 1, l, i, 4)

                act.wait_ge(blk_done, BLOCKS * l + B_M + 2)
                act.wait_ge(y_raw, DT * l + DT + 1)
                for k in range(DT):
                    A(YSH[:, k, :], YSF[:, k, :], ACT.Copy).then_inc(y_hi, 1)
                act.wait_ge(ya_out, 2 * DT * (l + 1) + 1)
                for k in range(DT):
                    A(YAH[:, k, :], YAF[:, k, :], ACT.Copy).then_inc(y_hi, 1)

                with act.Fori(0, NQ) as j:
                    n0 = 2 * (M_M - M_A)
                    ada_load(l, n0 + 4 * j, 1, l, M_M + 2 * j)
                    hi(B_M + 2, 0, l, j, 2)
                    for a in (2, 3):
                        ada_load(l, n0 + 4 * j, a, l, M_M + 2 * j + 1)
                    hi(B_M + 3, 1, l, j, 2)
                    ada_load(l, n0 + 4 * j, 4, l, M_M + 2 * j + 2)
                    act.wait_ge(m_sum, NQ * l + j + 1)
                    alone(act)
                    A(MH[:, ds(2 * j, 2), :], GA[:, ds(2 * j, 2), :], ACT.Copy).then_inc(m_hi, 1)

                def residual_squares(tile, block, s, use):
                    for a in range(2):
                        if a == 0:
                            act.wait_ge(x_ready, DT + DT * l + block + 1)
                        else:
                            act.wait_ge(bank_free[s], USES * l + use + 2)
                        act.wait_ge(sq_added, DT + 2 * DT * l + 2 * block + a - 1)
                        alone(act)
                        A(SQ[a][:], X[:, ds(tile + a, 1), :].rearrange("p o s -> p (o s)"),
                          ACT.Square).then_inc(sq_ready, 1)

                with act.Fori(0, 2) as i:
                    for s in range(2):
                        hi(B_O + 2 + s, s, l, i, 2)
                        residual_squares(i * 4 + 2 * s, i * 2 + s, s, U_O + i)
                norm_tiles(2 * l + 1)
                shifted(2 * l + 1)

                def ffn_iteration(j, with_ada):
                    if with_ada:
                        ada_load(l, 2 * (M_F - M_A) + 2 * j, 1, l, M_F + j)
                    act.wait_ge(f_lo, NF * l + j + 1)
                    act.wait_ge(blk_done, BLOCKS * l + B_F + j * 2 + 3)
                    for a in range(2):
                        alone(act)
                        A(CONVT[:, a:a + 1, :], PS[:, a:a + 1, :], ACT.Identity,
                          bias=VEC[:, ds(l, 1), 1, ds(CONV * FT + 2 * j + a, 1)].rearrange("p o r -> p (o r)"),
                          scale=VEC[:, ds(l, 1), 1, ds((CONV - 1) * FT + 2 * j + a, 1)].rearrange("p o r -> p (o r)")
                          ).then_inc(conv_pre, 1)
                    hi(B_F + 2, 0, l, j, 2)
                    act.wait_ge(bank_free[0], USES * l + U_F + j + 2)
                    A(CONVT[:], CONVT[:], ACT.Silu).then_inc(silu_done, 1)
                    act.wait_ge(bank_free[1], USES * l + U_F + j + 2)
                    alone(act)
                    A(FH[:, ds(2 * j, 2), :], CONVT[:], ACT.Copy).then_inc(f_hi, 1)
                    hi(B_F + 3, 1, l, j, 2)

                with act.Fori(0, DT - 1) as j:
                    ffn_iteration(j, True)
                    ada_load(l, 2 * (M_F - M_A) + 2 * j, 2, l, M_F + j + 1)
                ffn_iteration(DT - 1, True)
                with act.Fori(DT, NF) as j:
                    ffn_iteration(j, False)

                other = (DEPTH - 1) - l
                n0 = 2 * (M_D - M_A)
                ada_load(l, n0, 0, other, 0)
                ada_load(l, n0, 1, other, 0)
                for b in range(16):
                    if b + 2 < 16:
                        k0, k1 = SEGS[(b + 2) % 4]
                        hi(B_D + b + 2, b % 2, l, kts=k1 - k0)
                    if b + 1 < 16:
                        ada_load(l, n0, 2 * b + 2, other, b + 1)
                        ada_load(l, n0, 2 * b + 3, other, b + 1)
                    if b % 4 == 3:
                        g = b // 4
                        residual_squares(2 * g, NQ + g, g % 2, U_D + g // 2)

            norm_tiles(2 * DEPTH)
            for k in range(DT):
                act.wait_ge(out_trans, k + 1)
                A(OUT_T[:, :, k * P:(k + 1) * P], PS[:, k % 4, :].rearrange("p (b q) -> p b q", b=NB),
                  ACT.Copy).then_inc(out_copied, 1)

        @block.vector
        def _(dve):
            v = nc.vector
            dve.sem_inc(w_lo, 2)
            for s in range(2):
                dve.sem_inc(bank_free[s], 1)
            dve.sem_inc(y_raw, 1)
            dve.sem_inc(ada_used, 2)
            chain = Chain(dve, dve_chain)
            link = chain.link

            def lo(n, slot, l, kts=DT, width=BC):
                dve.wait_ge(w_hi, BLOCKS * l + n + 3)
                v.tensor_tensor(WL[:, slot, 0:kts, 0:width], WS[:, slot, 0:kts, 0:width],
                                WH[:, slot, 0:kts, 0:width], ALU.subtract).then_inc(w_lo, 1)

            def norm(nn, weight, shift, scale):
                link(v.tensor_copy(SHC[:], shift))
                link(v.scalar_tensor_tensor(WSC[:], scale, 1.0, weight, ALU.add, ALU.mult))
                dve.wait_ge(rms_root, nn + 1)
                link(v.reciprocal(RS[:], RS[:]))

                def pre(k):
                    v.scalar_tensor_tensor(NT[k % 2][:], X[:, k, :], WSC[:, k:k + 1], RS[:], ALU.mult,
                                           ALU.mult).then_inc(h_pre, 1)

                pre(0)
                pre(1)
                for k in range(DT):
                    dve.wait_ge(h_hi, DT * nn + k + 1)
                    v.scalar_tensor_tensor(HL[:, k, :], NT[k % 2][:], SHC[:, k:k + 1], HH[:, k, :], ALU.add,
                                           ALU.subtract).then_inc(h_lo, 1)
                    if k + 2 < DT:
                        dve.wait_ge(h_lo, DT * nn + k + 1)
                        pre(k + 2)

            def rotate(src, dst):
                alone(dve)
                half = ROT // 2
                v.stream_shuffle(ROTT[:], src, [(p + half) % ROT if p < ROT else p for p in range(32)])
                return v.tensor_tensor(dst, src, COS[:], ALU.mult)

            v.memset(EPSC[:], EPS).then_inc(ones_set, 1)
            dve.wait_ge(vec_ready, 1)
            dve.wait_ge(pos_in, 16)
            link(v.tensor_copy(T2[:], POS[:]))
            dve.wait_ge(const_in, 16)
            link(v.tensor_scalar(T1[:], T2[:], CST[:, C_FREQ:C_FREQ + 1], None, ALU.mult))
            for quarter, dst in ((0.0, SIN), (0.25, COS)):
                link(v.tensor_scalar(T2[:], T1[:], 1.0 / TWO_PI, quarter, ALU.mult, ALU.add))
                link(v.tensor_scalar(T3[:], T2[:], MAGIC, None, ALU.add))
                link(v.tensor_scalar(T2[:], T3[:], MAGIC, None, ALU.subtract))
                link(v.scalar_tensor_tensor(dst[:], T2[:], -TP1, T1[:], ALU.mult, ALU.add))
                link(v.scalar_tensor_tensor(dst[:], T2[:], -TP2, dst[:], ALU.mult, ALU.add))
                link(v.scalar_tensor_tensor(dst[:], T2[:], -TP3, dst[:], ALU.mult, ALU.add))
                if quarter:
                    link(v.tensor_scalar(dst[:], dst[:], math.pi / 2, None, ALU.add))
                link(v.tensor_scalar(dst[:], dst[:], PI_IN, -PI_IN, ALU.min, ALU.max))
            v.memset(T3[:], 0.0).then_inc(angle_ready, 1)
            dve.wait_ge(sine_ready, 2)
            link(v.tensor_scalar(SIN[:], SIN[:], CST[:, C_SIGN:C_SIGN + 1], None, ALU.mult))
            link(v.tensor_scalar(COS[:], COS[:], CST[:, C_ROT:C_ROT + 1], CST[:, C_PASS:C_PASS + 1],
                                 ALU.mult, ALU.add))
            dve.wait_ge(sinks_in, 16)
            dve.wait_ge(cact_ready, 1)
            dve.wait_ge(ada_cols, 1)
            v.tensor_tensor(MOD[:, 0, 0:2 * DT], PS[:, 7, 0:2 * DT], VEC[:, 0, 0, 0:2 * DT], ALU.add).then_inc(mod_ready, 1)
            dve.wait_ge(mod_ready, 1)

            with dve.Fori(0, DEPTH) as l:
                outer = chain.enter(l, LAYER_STEPS)
                lo(B_K, 0, l, width=P)
                lo(B_V, 1, l, width=P)

                def mod_cols(m0, r=l):
                    return MOD[:, ds(r, 1), m0:m0 + DT].rearrange("p o m -> p (o m)")

                def vec_cols(c0):
                    return VEC[:, ds(l, 1), 0, c0:c0 + DT].rearrange("p o m -> p (o m)")

                norm(2 * l, vec_cols(V_N1), mod_cols(0), mod_cols(DT))
                dve.wait_ge(blk_done, BLOCKS * l + B_K + 3)
                rotate(PS[:, 0, :], T3[:]).then_inc(bank_free[0], 1)
                lo(B_ZV, 0, l)
                lo(B_ZV + 1, 1, l)
                with dve.Fori(0, 2) as i:
                    for s in range(2):
                        lo(B_ZV + 2 + s + i * 2, s, l)
                dve.wait_ge(v_hi, l + 1)
                v.tensor_tensor(VL[:].rearrange("p b d -> p (b d)"), PS[:, 4, :],
                                VH[:].rearrange("p b d -> p (b d)"), ALU.subtract).then_inc(v_lo, 1)
                for b in range(NB):
                    dve.wait_ge(zt_copied, NB * l + b + 1)
                    v.bn_stats(BN[:, b, 0:6], VT[:, b, 0:S])
                    link(v.bn_stats(BN[:, b, 6:12], VT[:, b, S:D]))
                    alone(dve)
                    ins = v.bn_aggr(MV[:, b, :], BN[:, b, :])
                ins.then_inc(ln_var, 1)
                dve.wait_ge(ln_root, l + 1)
                v.reciprocal(RSV[:], SD[:]).then_inc(ln_ready, 1)

                def ada_half(l, n0, number, unit, acc):
                    half = number % 2
                    dve.wait_ge(ada_loaded[half], 16 * ((ADA_HALVES // 2) * l + unit + 1))
                    for k in range(4):
                        src, ck = ADA[:, half:half + 1, k, :], CACT[:, 4 * half + k:4 * half + k + 1]
                        if half == 0 and k == 0:
                            ins = v.tensor_scalar(acc, src, ck, None, ALU.mult)
                        else:
                            ins = v.scalar_tensor_tensor(acc, src, ck, acc, ALU.mult, ALU.add)
                        if k < 3:
                            link(ins)
                    ins.then_inc(ada_used, 1)
                    if half == 0:
                        dve.wait_ge(ada_used, ADA_HALVES * l + n0 + number + 3)

                def modulation(bank, col, layer, m0, n):
                    return v.tensor_tensor(MOD[:, ds(layer, 1), ds(m0, n)], PS[:, bank:bank + 1, col:col + n],
                                           VEC[:, ds(layer, 1), 0, ds(m0, n)], ALU.add)

                with dve.Fori(0, NQ) as i:
                    inner = chain.enter(i, ATTN_STEPS)
                    dve.wait_ge(blk_done, BLOCKS * l + B_Q + i * 4 + 3)
                    for t in range(2):
                        dve.wait_ge(rope_out, (DT + 1) * l + 2 * i + t + 1)
                        ins = rotate(PS[:, t, :], QF[:, t, :])
                        ins.then_inc(rope_cos if t == 0 else bank_free[0], 1)
                    link(v.tensor_copy(SINKC[:], SINK[:, ds(l, 1), :, ds(2 * i, 2)].rearrange("p o h t -> p (o h) t")))
                    for b in range(NB):
                        ins = v.tensor_scalar(VN[:, b:b + 1, :], VT[:, b:b + 1, ds(BC * i, BC)], MV[:, b, 0:1],
                                              RSV[:, b:b + 1], ALU.subtract, ALU.mult)
                    ins.then_inc(vn_ready, 1)
                    lo(B_Q + 2 + i * 4, 0, l)
                    dve.wait_ge(mixw_trans, NQ * l + i + 2)
                    v.tensor_copy(WT[:].rearrange("p g t -> p (g t)"), PS[:, 6, 0:2 * P]).then_inc(mixw_ready, 1)
                    units = NB * DT * l + NB * 2 * i

                    def mask_and_max(u):
                        t, b = u // NB, u % NB
                        first = 0 if b else P
                        dve.wait_ge(s_ready, units + u + 1)
                        if u >= 2:
                            dve.wait_ge(pt_ready, units + u - 1)
                        v.tensor_copy(SM[u % 2][:, :, 2 * P:2 * P + 1], SINKC[:, :, t:t + 1])
                        for h in range(KV_HEADS):
                            ins = v.tensor_tensor_reduce(
                                out=SM[u % 2][:, h, first:2 * P],
                                in0=PS[:, 4 + u % 2, h * 2 * P:h * 2 * P + 2 * P - first],
                                in1=CST[:, C_MASK + first:C_MASK + 2 * P], scale=HD ** -0.5,
                                scalar=SINKC[:, h, t:t + 1],
                                op0=ALU.add, op1=ALU.max, accum_out=MX[:, u % 2, h:h + 1])
                        ins.then_inc(s_used, 1)
                        dve.wait_ge(s_used, units + u + 1)
                        v.tensor_scalar(NM[:, u % 2, :], MX[:, u % 2, :], -1.0, None, ALU.mult).then_inc(nm_ready, 1)

                    def inverse(u):
                        dve.wait_ge(p_ready, units + u + 1)
                        v.reciprocal(RDEN[:, u % 2, :], DEN[:, u % 2, :]).then_inc(rden_ready, 1)

                    def prob_lo(u):
                        first = 0 if u % NB else 1
                        dve.wait_ge(pt_hi, units + u + 1)
                        v.tensor_tensor(PTL[:, first:2].rearrange("p k h q -> p (k h q)"), PS[:, 6, first * 2 * P:],
                                        PTH[:, first:2].rearrange("p k h q -> p (k h q)"),
                                        ALU.subtract).then_inc(pt_lo, 1)

                    for w in range(11):
                        if w < 8:
                            mask_and_max(w)
                        if w == 0:
                            dve.wait_ge(rowsum_ready, NQ * l + i + 1)
                            dve.wait_ge(mixb_loaded, 16 * (NQ * l + i + 1))
                            for g in range(2):
                                lnb = VEC[:, ds(l, 1), 0, ds(V_LNB + 2 * i + g, 1)].rearrange("p o r -> p (o r)")
                                ins = v.scalar_tensor_tensor(RB[:, g, :], PS[:, 6, g * P:(g + 1) * P], lnb,
                                                             RB[:, g, :], ALU.mult, ALU.add)
                            ins.then_inc(mixb_ready, 1)
                        if w < 8:
                            inverse(w)
                        if 0 <= w - 2 < 8:
                            prob_lo(w - 2)
                        if w < 8:
                            ada_half(l, 8 * i, w, 4 * i + w // 2, ADA_ACCA[:, w // 2:w // 2 + 1, :])
                        if w == 3:
                            lo(B_Q + 3 + i * 4, 1, l)
                        if w == 7:
                            lo(B_Q + 4 + i * 4, 0, l)
                    dve.wait_ge(mixb_ready, NQ * l + i + 1)
                    for g in range(2):
                        lnw = VEC[:, ds(l, 1), 0, ds(V_LNW + 2 * i + g, 1)].rearrange("p o r -> p (o r)")
                        dve.wait_ge(mixed, 2 * (NQ * l + i) + g + 1)
                        m = PS[:, 4 + g, :].rearrange("p (b t) -> p b t", b=NB)
                        link(v.scalar_tensor_tensor(m, m, lnw, RB[:, g:g + 1, :].to_broadcast([P, NB, P]),
                                                    ALU.mult, ALU.add))
                        dve.wait_ge(bank_free[1], USES * l + U_Q + 2 * i + 2)
                        v.tensor_tensor(YSF[:, ds(2 * i + g, 1), :], PS[:, 4 + g:5 + g, :],
                                        YSF[:, ds(2 * i + g, 1), :], ALU.mult).then_inc(y_raw, 1)
                    dve.wait_ge(ada_cols, MOD_SUMS * l + i + 2)
                    modulation(6, 0, l, M_A + 4 * i, 4).then_inc(mod_ready, 1)
                    lo(B_Q + 5 + i * 4, 1, l)
                    chain.leave(inner, NQ)

                for k in range(DT):
                    dve.wait_ge(y_hi, 2 * DT * l + k + 1)
                    v.tensor_tensor(YSL[:, k, :], YSF[:, k, :], YSH[:, k, :], ALU.subtract).then_inc(y_lo, 1)
                for k in range(DT):
                    dve.wait_ge(y_hi, 2 * DT * l + DT + k + 1)
                    v.tensor_tensor(YAL[:, k, :], YAF[:, k, :], YAH[:, k, :], ALU.subtract).then_inc(y_lo, 1)

                with dve.Fori(0, NQ) as j:
                    inner = chain.enter(j, MERGE_STEPS)

                    def halves(first):
                        for a in (first, first + 1):
                            ada_half(l, 2 * (M_M - M_A) + 4 * j, a, M_M - M_A + 2 * j + a // 2,
                                     ADA_ACCM[:, ds(2 * j + a // 2, 1), :])

                    halves(0)
                    dve.wait_ge(blk_done, BLOCKS * l + B_M + j * 2 + 3)
                    v.tensor_tensor(GA[:, ds(2 * j, 2), :], bank_pair(0), GA[:, ds(2 * j, 2), :],
                                    ALU.mult).then_inc(bank_free[0], 1)
                    lo(B_M + 2 + j * 2, 0, l)
                    halves(2)
                    dve.wait_ge(blk_done, BLOCKS * l + B_M + j * 2 + 1 + 3)
                    v.tensor_tensor(GB[:, ds(2 * j, 2), :], bank_pair(1), GB[:, ds(2 * j, 2), :],
                                    ALU.mult).then_inc(bank_free[1], 1)
                    lo(B_M + 3 + j * 2, 1, l)
                    dve.wait_ge(m_hi, NQ * l + j + 1)
                    v.tensor_tensor(ML[:, ds(2 * j, 2), :], GA[:, ds(2 * j, 2), :], MH[:, ds(2 * j, 2), :],
                                    ALU.subtract).then_inc(m_lo, 1)
                    chain.leave(inner, NQ)
                dve.wait_ge(ada_cols, MOD_SUMS * l + NQ + 2)
                modulation(7, 0, l, M_M, DT).then_inc(mod_ready, 1)

                def add_residual(slot, tile, gate):
                    for a in range(2):
                        g = MOD[:, ds(l, 1), ds(gate + tile + a, 1)].rearrange("p o m -> p (o m)")
                        xt = X[:, ds(tile + a, 1), :]
                        v.scalar_tensor_tensor(xt, PS[:, 2 * slot + a:2 * slot + a + 1, :], g, xt, ALU.mult,
                                               ALU.add).then_inc(bank_free[slot] if a else x_ready, 1)

                dve.wait_ge(mod_ready, MOD_SUMS * l + NQ + 2)
                alone(dve)
                with dve.Fori(0, 2) as i:
                    for s in range(2):
                        dve.wait_ge(blk_done, BLOCKS * l + B_O + i * 2 + s + 3)
                        add_residual(s, i * 4 + 2 * s, 2 * DT)
                        lo(B_O + 2 + s + i * 2, s, l)

                norm(2 * l + 1, vec_cols(V_N2), mod_cols(3 * DT), mod_cols(4 * DT))

                def ffn_iteration(j, with_ada):
                    for a in range(2):
                        dve.wait_ge(conv_pre, 2 * (NF * l + j) + a + 1)
                        for tap in (1, 0):
                            lag = CONV - 1 - tap
                            wt = VEC[:, ds(l, 1), 1, ds(tap * FT + 2 * j + a, 1)].rearrange("p o r -> p (o r)")
                            dst = CONVT[:, a:a + 1, lag:]
                            ins = v.scalar_tensor_tensor(dst, PS[:, a:a + 1, 0:S - lag], wt, dst, ALU.mult, ALU.add)
                            if not (a == 1 and tap == 0):
                                link(ins)
                    ins.then_inc(bank_free[0], 1)
                    lo(B_F + 2 + j * 2, 0, l)
                    if with_ada:
                        for a in range(2):
                            ada_half(l, 2 * (M_F - M_A) + 2 * j, a, M_F - M_A + j, ADA_ACCF[:, ds(j, 1), :])
                    dve.wait_ge(silu_done, NF * l + j + 1)
                    dve.wait_ge(blk_done, BLOCKS * l + B_F + j * 2 + 1 + 3)
                    v.tensor_tensor(CONVT[:], CONVT[:], bank_pair(1), ALU.mult).then_inc(bank_free[1], 1)
                    lo(B_F + 3 + j * 2, 1, l)

                with dve.Fori(0, DT) as j:
                    inner = chain.enter(j, FFN_STEPS[0])
                    ffn_iteration(j, True)
                    chain.leave(inner, DT)
                with dve.Fori(DT, NF) as j:
                    inner = chain.enter(j - DT, FFN_STEPS[1])
                    ffn_iteration(j, False)
                    chain.leave(inner, NF - DT)
                dve.wait_ge(ada_cols, MOD_SUMS * l + NQ + 3)
                modulation(7, 0, l, M_F, DT).then_inc(mod_ready, 1)
                dve.wait_ge(mod_ready, MOD_SUMS * l + NQ + 3)

                for b in range(16):
                    for a in range(2):
                        ada_half(l, 2 * (M_D - M_A), 2 * b + a, M_D - M_A + b, ADA_ACCD[:, b:b + 1, :])
                    if b % 4 == 3:
                        dve.wait_ge(blk_done, BLOCKS * l + B_D + b + 3)
                        add_residual((b // 4) % 2, b // 4 * 2, M_F)
                    if b + 2 < 16:
                        k0, k1 = SEGS[(b + 2) % 4]
                        lo(B_D + b + 2, b % 2, l, kts=k1 - k0)
                dve.wait_ge(ada_cols, MOD_SUMS * l + NQ + 4)
                alone(dve)
                modulation(7, 0, (DEPTH - 1) - l, 0, 2 * DT).then_inc(mod_ready, 1)
                dve.wait_ge(mod_ready, MOD_SUMS * l + NQ + 4)
                chain.leave(outer, DEPTH)

            dve.wait_ge(rms_root, 2 * DEPTH + 1)
            link(v.reciprocal(RS[:], RS[:]))
            for k in range(DT):
                dst = FIN[k % 2][:, k // 2, :]
                v.scalar_tensor_tensor(dst, X[:, k, :], VEC[:, 0, 0, V_EXTRA + k:V_EXTRA + k + 1], RS[:], ALU.mult,
                                       ALU.mult).then_inc(fin_tile, 1)

        @block.gpsimd
        def _(pool):
            g_ = nc.gpsimd
            chain = Chain(pool, pool_chain)
            link = chain.link
            pool.sem_inc(f_lo, 1)
            g_.memset(ONES[:], 1.0).then_inc(ones_set, 1)

            def add_square(nn_count, src):
                pool.wait_ge(sq_ready, nn_count + 1)
                g_.tensor_tensor(ACC[:], ACC[:], src, ALU.add).then_inc(sq_added, 1)
                pool.wait_ge(sq_added, nn_count + 1)

            pool.wait_ge(angle_ready, 1)
            g_.memset(ACC[:], 0.0).then_inc(acc_zero, 1)
            pool.wait_ge(acc_zero, 1)
            for k in range(DT):
                add_square(k, SQ0[k % 2][:])
            pool.wait_ge(x_ready, DT)

            with pool.Fori(0, DEPTH) as l:
                outer = chain.enter(l, POOL_LAYER_STEPS)

                pool.wait_ge(stat_ready, 2 * l + 1)
                alone(pool)
                link(g_.memset(KP[HD:P, 0, :], 0.0))
                alone(pool)
                link(g_.memset(KP[0:HD, 1, :], 0.0))
                pool.wait_ge(bank_free[0], USES * l + 2)
                link(g_.tensor_tensor(ROTT[:], ROTT[:], SIN[:], ALU.mult))
                for h in range(KV_HEADS):
                    rows = slice(h * HD, (h + 1) * HD)
                    ins = g_.tensor_tensor(KP[rows, h, :], T3[rows, :], ROTT[rows, :], ALU.add)
                ins.then_inc(rope_out, 1)

                def turn(f):
                    link(g_.tensor_tensor(ROTT[:], ROTT[:], SIN[:], ALU.mult))
                    g_.tensor_tensor(f, f, ROTT[:], ALU.add).then_inc(rope_out, 1)

                pool.wait_ge(ln_ready, l + 1)
                alone(pool)
                with pool.Fori(0, NQ) as i:
                    inner = chain.enter(i, 2)
                    pool.wait_ge(rope_cos, NQ * l + i + 1)
                    turn(QF[:, 0, :])
                    pool.wait_ge(bank_free[0], USES * l + U_Q + 2 * i + 2)
                    turn(QF[:, 1, :])
                    pool.wait_ge(mixw_loaded, 16 * (NQ * l + i + 1))
                    alone(pool)
                    g_.affine_select(out=WRAW[:], in_=WRAW[:], compare_op=ALU.is_ge, fill=0.0, base=0,
                                     pattern=[[0, 2], [-1, P]], channel_multiplier=1).then_inc(mixw_causal, 1)
                    units = NB * DT * l + NB * 2 * i
                    for u in range(8):
                        first = 0 if u % NB else P
                        pool.wait_ge(rden_ready, units + u + 1)
                        alone(pool)
                        for h in range(KV_HEADS):
                            cols = SM[u % 2][:, h, first:2 * P]
                            ins = g_.tensor_scalar(cols, cols, RDEN[:, u % 2, h:h + 1], None, ALU.mult)
                        ins.then_inc(pn_ready, 1)
                    chain.leave(inner, NQ)
                with pool.Fori(0, NQ) as j:
                    pool.wait_ge(bank_free[1], USES * l + U_M + j + 2)
                    g_.tensor_tensor(GA[:, ds(2 * j, 2), :], GA[:, ds(2 * j, 2), :], GB[:, ds(2 * j, 2), :],
                                     ALU.add).then_inc(m_sum, 1)

                def sum_squares(nn):
                    pool.wait_ge(stat_ready, nn)
                    alone(pool)
                    link(g_.memset(ACC[:], 0.0))
                    alone(pool)
                    with pool.Fori(0, DT // 2) as m:
                        for a in range(2):
                            add_square(DT * nn + 2 * m + a, SQ[a][:])

                sum_squares(2 * l + 1)
                with pool.Fori(0, NF) as j:
                    pool.wait_ge(f_hi, NF * l + j + 1)
                    g_.tensor_tensor(FL[:, ds(2 * j, 2), :], CONVT[:], FH[:, ds(2 * j, 2), :],
                                     ALU.subtract).then_inc(f_lo, 1)
                sum_squares(2 * l + 2)
                chain.leave(outer, DEPTH)


LAYER_STEPS, ATTN_STEPS, MERGE_STEPS, FFN_STEPS, POOL_LAYER_STEPS = 343, 27, 12, (9, 3), 13

_INS = ["x", "c", "positions", "ada_w", "ada_b", "norm1_w", "w_in", "attn_sinks", "sgu_ln_w", "sgu_ln_b", "sgu_w",
        "sgu_b", "proj_a", "proj_b", "w_out", "norm2_w", "ffn_w_gate", "ffn_w_up", "ffn_conv_w", "ffn_conv_b",
        "ffn_w_down", "final_norm_w"]


def kernel(**inputs):
    import concourse.bacc as _bacc
    from concourse.bass_utils import run_bass_kernel_spmd as _run

    nc = _bacc.Bacc("TRN2", target_bir_lowering=False, num_devices=1, dynamic_dma_scratch_size=64)
    arrays, args = {}, []
    for name in _INS:
        a = np.ascontiguousarray(inputs[name])
        arrays[f"in_{name}"] = a
        args.append(nc.dram_tensor(f"in_{name}", a.shape, mybir.dt.from_np(a.dtype), kind="ExternalInput").ap())
    a = shape_constants()
    arrays["shape_constants"] = a
    args.append(nc.dram_tensor("shape_constants", a.shape, F32, kind="ExternalInput").ap())
    args.append(nc.dram_tensor("out", (1, S, D), F32, kind="ExternalOutput").ap())
    trunk_kernel(nc, *args)
    r = _run(nc, [arrays], core_ids=[0])
    return r.results[0]["out"]
```

```python
import math
from contextlib import ExitStack

import numpy as np

import concourse.bass as bass
from concourse import mybir
from concourse.alu_op_type import AluOpType as ALU

F32 = mybir.dt.float32
F32R = mybir.dt.float32r
I32 = mybir.dt.int32
ACT = mybir.ActivationFunctionType
ds = bass.ds

P = 128
D = 1024
S = 512
DEPTH = 2
HEADS = 16
KV_HEADS = 2
HD = 64
ROT = HD // 4
WINDOW = 128
THETA = 500000.0
SGU = 1024
FFN = 2816
CONV = 3
EPS = 1e-6

DT = D // P
NB = S // P
NQ = DT // 2
FT = FFN // P
BC = 2 * P
Q_END = HEADS * HD
K_END = Q_END + KV_HEADS * HD
V_END = K_END + KV_HEADS * HD
U_END = V_END + SGU
Z_END = U_END + SGU
HALF_Q = Q_END // 2

PE0, SUMS0, POOL0 = (2, 6), (0, 1, 3, 5, 7), (4,)

B_K, B_V = 0, 1
W_INC = 64
B_ZV = 2
B_Q = B_ZV + 4
B_M = B_Q + 16
B_O = B_M + 8
B_F = B_O + 4
B_D = B_F + 2 * (FT // 2)
BLOCKS = B_D + 16
SEGS = [(0, 6), (6, 12), (12, 17), (17, 22)]
NF = FT // 2

U_ZV, U_Q, U_M, U_O, U_F, U_D, USES = 1, 3, 11, 15, 17, 28, 30

N_MOD = 6 * DT
ADA_HALVES = 2 * N_MOD
M_A, M_M, M_F, M_D = 2 * DT, 4 * DT, 5 * DT, 6 * DT
MOD_SUMS = NQ + 3
ADA_SUMS = {1: 2, 2: 3, 3: 4, 5: 5, 6: 6, 7: 7}
ADA_LOADS = {2: 4, 3: 5, 4: 6, 6: 7, 7: 8, 8: 9}

V_ADAB, V_N1, V_N2, V_LNW, V_LNB, V_EXTRA = 0, 48, 56, 64, 72, 80
VROWS = 88

MAGIC = 1.5 * 2.0 ** 23
TWO_PI = 2.0 * math.pi
TP1 = float(np.float32(6.28125))
TP2 = float(np.float32(np.float32((TWO_PI - TP1) * 2 ** 20).astype(np.int32) / 2.0 ** 20))
TP3 = float(np.float32(TWO_PI - TP1 - TP2))
PI_IN = float(np.nextafter(np.float32(math.pi), np.float32(0)))

NEG = -1.0e30

C_IDENT, C_MASK, C_FREQ, C_SIGN, C_ROT, C_PASS, C_END = 0, 128, 384, 385, 386, 387, 388


def shape_constants():
    c = np.zeros((P, C_END), np.float32)
    c[:, C_IDENT:C_IDENT + P] = np.eye(P, dtype=np.float32)
    i, j = np.arange(P)[:, None], np.arange(2 * P)[None, :]
    band = (j > i + P - WINDOW) & (j <= i + P)
    c[:, C_MASK:C_MASK + 2 * P] = np.where(band, 0.0, NEG)
    inv = (np.float32(THETA) ** (-np.arange(0, ROT, 2, dtype=np.float32) / np.float32(ROT))).astype(np.float32)
    d = np.arange(P) % HD
    c[:, C_FREQ] = np.where(d < ROT, inv[d % (ROT // 2)], 0.0)
    c[:, C_SIGN] = np.where(d < ROT // 2, -1.0, np.where(d < ROT, 1.0, 0.0))
    c[:, C_ROT] = d < ROT
    c[:, C_PASS] = d >= ROT
    return c


class Chain:

    def __init__(self, eng, sem):
        self.eng, self.sem, self.base, self.n = eng, sem, 0, 0

    def link(self, ins):
        ins.then_inc(self.sem, 1)
        self.n += 1
        self.eng.wait_ge(self.sem, self.base + self.n)

    def enter(self, reg, steps):
        held = (self.base, self.n, steps)
        self.base, self.n = self.base + self.n + reg * steps, 0
        return held

    def leave(self, held, times):
        base, n, steps = held
        assert self.n == steps, f"this loop's body has {self.n} steps, not {steps}"
        self.base, self.n = base, n + times * steps


def trunk_kernel(nc, x, c, positions, ada_w, ada_b, norm1_w, w_in, attn_sinks, sgu_ln_w, sgu_ln_b, sgu_w,
                 sgu_b, proj_a, proj_b, w_out, norm2_w, ffn_w_gate, ffn_w_up, ffn_conv_w, ffn_conv_b,
                 ffn_w_down, final_norm_w, consts, out):
    KB = 1024
    start = 192

    def at(name, shape, dtype, offset):
        return nc.alloc_sbuf_tensor_at(name, shape, dtype, offset=offset)

    o = start
    X = at("X", [P, DT, S], F32, o); o += 16 * KB
    HH = at("HH", [P, DT, S], F32R, o)
    HL = at("HL", [P, DT, S], F32R, o + 16 * KB)
    ADA_ACC0 = at("ADA_ACC0", [P, DT, BC], F32, o)
    YSH = at("YSH", [P, DT, S], F32R, o)
    YSL = at("YSL", [P, DT, S], F32R, o + 16 * KB)
    OUT_T = at("OUT_T", [P, NB, D], F32, o + 16 * KB)
    o += 32 * KB
    big = o
    FH = at("FH", [P, FT, S], F32R, big)
    FL = at("FL", [P, FT, S], F32R, big + 44 * KB)
    ADA0 = at("ADA0", [P, DT, DT, BC], F32, big)
    YAF = at("YAF", [P, DT, S], F32, big)
    YAL = at("YAL", [P, DT, S], F32R, big)
    YSF = at("YSF", [P, DT, S], F32, big + 16 * KB)
    FIN = [at(f"FIN{n}", [P, 4, S], F32, big + n * 8 * KB) for n in range(2)]
    GA = at("GA", [P, DT, S], F32, big + 32 * KB)
    ML = at("ML", [P, DT, S], F32R, big + 32 * KB)
    GB = at("GB", [P, DT, S], F32, big + 48 * KB)
    MH = at("MH", [P, DT, S], F32R, big + 48 * KB)
    v0 = big + 64 * KB
    QF = at("QF", [P, 2, S], F32, v0)
    PTH = at("PTH", [P, 2, 2, P], F32R, v0 + 4 * KB)
    PTL = at("PTL", [P, 2, 2, P], F32R, v0 + 6 * KB)
    WRAW = at("WRAW", [P, 2, P], F32, v0 + 8 * KB)
    WT = at("WT", [P, 2, P], F32, v0 + 9 * KB)
    RB = at("RB", [P, 2, P], F32, v0 + 10 * KB)
    SM = [at(f"SM{n}", [P, 2, 2 * P + 1], F32, v0 + 11 * KB + n * 2080) for n in range(2)]
    ADA_ACCM = at("ADA_ACCM", [P, DT, P], F32, v0)
    k0 = v0 + 16 * KB
    KP = at("KP", [P, KV_HEADS, S], F32, k0)
    VH = at("VH", [P, NB, P], F32R, k0 + 4 * KB)
    VL = at("VL", [P, NB, P], F32R, k0 + 6 * KB)
    o += 88 * KB
    e0 = o
    XT = at("XT", [P, NB, D], F32, e0)
    VT = at("VT", [P, NB, D], F32, e0)
    YAH = at("YAH", [P, DT, S], F32R, e0)
    CONVT = at("CONVT", [P, 2, S], F32, e0)
    ADA_ACCF = at("ADA_ACCF", [P, DT, P], F32, e0 + 4 * KB)
    ADA_ACCD = at("ADA_ACCD", [P, 2 * DT, P], F32, e0 + 8 * KB)
    o += 16 * KB
    WS = at("WS", [P, 2, DT, BC], F32, o); o += 16 * KB
    WH = at("WH", [P, 2, DT, BC], F32R, o); o += 16 * KB
    WL = at("WL", [P, 2, DT, BC], F32R, o); o += 16 * KB
    t0 = o
    VN = at("VN", [P, NB, BC], F32, t0)
    ADA_ACCA = at("ADA_ACCA", [P, 4, P], F32, t0 + 6 * KB)
    VRAW = at("VRAW", [P, S], F32, t0)
    SQ0 = [at(f"SQ0{n}", [P, S], F32, k0 + n * 2 * KB) for n in range(2)]
    DIAG = at("DIAG", [P, NB, P], F32, t0)
    VR = at("VR", [VROWS, 4, P], F32, t0)
    T1 = at("T1", [P, S], F32, t0 + 2 * KB)
    T2 = at("T2", [P, S], F32, t0 + 4 * KB)
    T3 = at("T3", [P, S], F32, t0 + 6 * KB)
    POS = at("POS", [P, S], I32, t0 + 2 * KB)
    ROTT = T2
    ACC = at("ACC", [P, S], F32, t0 + 4 * KB)
    SQ = [T1, T3]
    NT = [T1, T3]
    o += 8 * KB
    ADA = at("ADA", [P, 2, 4, P], F32, o); o += 4 * KB
    COS = at("COS", [P, S], F32, o); o += 2 * KB
    SIN = at("SIN", [P, S], F32, o); o += 2 * KB
    CST = at("CST", [P, C_END], F32, o); o += 1568
    ONES = at("ONES", [P, P], F32, o); o += 512
    VEC = at("VEC", [P, DEPTH, 2, VROWS], F32, o); o += 1408
    MOD = at("MOD", [P, DEPTH, N_MOD], F32, o); o += 384
    SINK = at("SINK", [P, DEPTH, KV_HEADS, HEADS // 2], F32, o); o += 128
    SINKC = at("SINKC", [P, KV_HEADS, 2], F32, o); o += 32
    CACT = at("CACT", [P, DT], F32, o); o += 32
    WSC = at("WSC", [P, DT], F32, o); o += 32
    SHC = at("SHC", [P, DT], F32, o); o += 32
    MX = at("MX", [P, 2, 2], F32, o); o += 32
    NM = at("NM", [P, 2, 2], F32, o); o += 32
    DEN = at("DEN", [P, 2, 2], F32, o); o += 32
    RDEN = at("RDEN", [P, 2, 2], F32, o); o += 32
    BN = at("BN", [P, NB, 24], F32, o); o += 384
    MV = at("MV", [P, NB, 2], F32, o); o += 32
    SD = at("SD", [P, NB], F32, o); o += 32
    RSV = at("RSV", [P, NB], F32, o); o += 32
    EPSC = at("EPSC", [P, 1], F32, o); o += 32
    RMS = at("RMS", [P, NB], F32, o); o += 32
    assert o <= nc.sbuf_usable_end, (o, nc.sbuf_usable_end)
    IDENT = CST[:, C_IDENT:C_IDENT + P]

    w_in_v = w_in.rearrange("l (k p) n -> p l k n", p=P)
    proj_a_v = proj_a.rearrange("l (k p) n -> p l k n", p=P)
    proj_b_v = proj_b.rearrange("l (s k p) n -> s p l k n", s=KV_HEADS, p=HD)
    w_out_v = w_out.rearrange("l (k p) n -> p l k n", p=P)
    gate_v = ffn_w_gate.rearrange("l (k p) n -> p l k n", p=P)
    up_v = ffn_w_up.rearrange("l (k p) n -> p l k n", p=P)
    down_v = ffn_w_down.rearrange("l (k p) n -> p l k n", p=P)
    ada_v = ada_w.rearrange("l (k p) n -> p l k n", p=P)
    sgu_w_v = sgu_w.rearrange("l g t s -> t l g s")

    with ExitStack() as ctx:
        def sem(name):
            return ctx.enter_context(nc.semaphore(name))

        PS = ctx.enter_context(nc.psum_tensor("PS", [P, 8, S], F32))

        w_loaded = [sem("w_loaded0"), sem("w_loaded1")]
        w_hi = sem("w_hi")
        w_lo = sem("w_lo")
        blk_done = sem("blk_done")
        bank_free = [sem("bank_free0"), sem("bank_free1")]
        sq_ready = sem("sq_ready")
        x_ready = sem("x_ready")
        acc_zero = sem("acc_zero")
        sq_added = sem("sq_added")
        stat_ready = sem("stat_ready")
        rms_root = sem("rms_root")
        rms_diag = sem("rms_diag")
        rms_wide = sem("rms_wide")
        h_pre = sem("h_pre")
        h_hi = sem("h_hi")
        h_lo = sem("h_lo")
        rope_cos = sem("rope_cos")
        rope_out = sem("rope_out")
        v_trans = sem("v_trans")
        v_hi = sem("v_hi")
        v_lo = sem("v_lo")
        ln_var = sem("ln_var")
        ln_root = sem("ln_root")
        ln_ready = sem("ln_ready")
        mixw_loaded = sem("mixw_loaded")
        mixb_loaded = sem("mixb_loaded")
        mixw_causal = sem("mixw_causal")
        mixw_trans = sem("mixw_trans")
        mixw_ready = sem("mixw_ready")
        rowsum_ready = sem("rowsum_ready")
        mixb_ready = sem("mixb_ready")
        vn_ready = sem("vn_ready")
        mixed = sem("mixed")
        y_raw = sem("y_raw")
        y_hi = sem("y_hi")
        y_lo = sem("y_lo")
        s_ready = sem("s_ready")
        s_used = sem("s_used")
        nm_ready = sem("nm_ready")
        p_ready = sem("p_ready")
        rden_ready = sem("rden_ready")
        pn_ready = sem("pn_ready")
        pt_ready = sem("pt_ready")
        pt_hi = sem("pt_hi")
        pt_lo = sem("pt_lo")
        o_ready = sem("o_ready")
        ya_out = sem("ya_out")
        m_sum = sem("m_sum")
        m_hi = sem("m_hi")
        m_lo = sem("m_lo")
        ada_loaded = [sem(f"ada_loaded{n}") for n in range(2)]
        ada_used = sem("ada_used")
        ada_cols = sem("ada_cols")
        mod_ready = sem("mod_ready")
        conv_pre = sem("conv_pre")
        silu_done = sem("silu_done")
        f_hi = sem("f_hi")
        f_lo = sem("f_lo")
        waits_passed = sem("waits_passed")
        dve_chain = sem("dve_chain")
        pool_chain = sem("pool_chain")
        const_in = sem("const_in")
        x_in = sem("x_in")
        rows_in = sem("rows_in")
        sinks_in = sem("sinks_in")
        pos_in = sem("pos_in")
        ada0_in = [sem(f"ada0_in{n}") for n in range(DT)]
        ones_set = sem("ones_set")
        vec_trans = sem("vec_trans")
        vec_ready = sem("vec_ready")
        x_trans = sem("x_trans")
        cact_ready = sem("cact_ready")
        ada0_sum = sem("ada0_sum")
        ada0_pool = sem("ada0_pool")
        angle_ready = sem("angle_ready")
        sine_ready = sem("sine_ready")
        fin_tile = sem("fin_tile")
        out_trans = sem("out_trans")
        out_copied = sem("out_copied")
        out_stored = sem("out_stored")

        block = ctx.enter_context(nc.Block())

        def alone(eng):
            eng.sem_inc(waits_passed, 1)

        def bank_pair(s):
            return PS[:, 2 * s:2 * s + 2, :]

        def load_rows(queue, l):
            for src, r0, n in ((ada_b, V_ADAB, 48), (norm1_w, V_N1, 8), (norm2_w, V_N2, 8),
                               (sgu_ln_w, V_LNW, 8), (sgu_ln_b, V_LNB, 8)):
                queue.dma_start(VR[r0:r0 + n, 2 * l, :], src[l].rearrange("(r p) -> r p", p=P)).then_inc(rows_in, 16)
            queue.dma_start(VR[0:CONV * FT, 2 * l + 1, :],
                            ffn_conv_w[l].rearrange("t (r p) -> (t r) p", p=P)).then_inc(rows_in, 16)
            queue.dma_start(VR[CONV * FT:VROWS, 2 * l + 1, :],
                            ffn_conv_b[l].rearrange("(r p) -> r p", p=P)).then_inc(rows_in, 16)

        @block.sync
        def _(sp):
            sp.dma_start(CST[:], consts).then_inc(const_in, 16)
            sp.dma_start(POS[:], positions.to_broadcast([P, S])).then_inc(pos_in, 16)
            load_rows(sp, 1)
            sp.dma_start(XT[:], x[0].rearrange("(b p) d -> p b d", p=P)).then_inc(x_in, 16)
            sp.wait_ge(rows_in, 16 * (7 * DEPTH + 2))
            for n in range(DT):
                sp.dma_start(ADA0[:, n], ada_v[:, 0, :, n * BC:(n + 1) * BC]).then_inc(ada0_in[n], 16)
            sp.dma_start(SINK[:], attn_sinks.rearrange("l h -> (l h)")[None, :].to_broadcast([P, DEPTH * HEADS])
                         .rearrange("p (l s h) -> p l s h", l=DEPTH, s=KV_HEADS)).then_inc(sinks_in, 16)

            with sp.Fori(0, DEPTH) as l:
                def load(n, slot, parts):
                    sp.wait_ge(w_lo, BLOCKS * l + n + 1)
                    for dst, src in parts:
                        sp.dma_start(dst, src).then_inc(w_loaded[slot], W_INC // len(parts))

                def load_block(n, slot, view, c0, k0=0, k1=DT, width=BC):
                    load(n, slot, [(WS[:, slot:slot + 1, 0:k1 - k0, 0:width],
                                    view[:, ds(l, 1), k0:k1, ds(c0, width)])])

                load_block(B_K, 0, w_in_v, Q_END, width=P)
                load_block(B_V, 1, w_in_v, K_END, width=P)
                with sp.Fori(0, 2) as i:
                    for s in range(2):
                        load_block(B_ZV + i * 2 + s, s, w_in_v, U_END + (i * 2 + s) * BC)
                with sp.Fori(0, NQ) as i:
                    load(B_Q + i * 4, 0, [(WS[:, 0:1, :, (2 * t + h) * HD:(2 * t + h + 1) * HD],
                                           w_in_v[:, ds(l, 1), :, ds(h * HALF_Q + t * HD + i * P, HD)])
                                          for t in range(2) for h in range(KV_HEADS)])
                    load_block(B_Q + i * 4 + 1, 1, w_in_v, Z_END + i * BC)
                    sp.wait_ge(mixw_trans, NQ * l + i + 1)
                    sp.dma_start(WRAW[:, None], sgu_w_v[:, ds(l, 1), ds(2 * i, 2), :]).then_inc(mixw_loaded, 16)
                    sp.wait_ge(y_raw, 2 * (NQ * l + i) + 1)
                    sp.dma_start(RB[:], sgu_b[ds(l, 1), ds(2 * i, 2), :].to_broadcast([P, 2, P])).then_inc(mixb_loaded, 16)
                    load_block(B_Q + i * 4 + 2, 0, w_in_v, Z_END + D + i * BC)
                    load_block(B_Q + i * 4 + 3, 1, w_in_v, V_END + i * BC)
                with sp.Fori(0, NQ) as j:
                    load_block(B_M + j * 2, 0, proj_a_v, j * BC)
                    load(B_M + j * 2 + 1, 1, [(WS[h * HD:(h + 1) * HD, 1:2, :, :],
                                               proj_b_v[h][:, ds(l, 1), :, ds(j * BC, BC)]) for h in range(KV_HEADS)])
                with sp.Fori(0, 2) as i:
                    for s in range(2):
                        load_block(B_O + i * 2 + s, s, w_out_v, (i * 2 + s) * BC)
                with sp.Fori(0, NF) as j:
                    load_block(B_F + j * 2, 0, gate_v, j * BC)
                    load_block(B_F + j * 2 + 1, 1, up_v, j * BC)
                with sp.Fori(0, NQ) as g:
                    for n, (k0, k1) in enumerate(SEGS):
                        load_block(B_D + g * 4 + n, n % 2, down_v, g * BC, k0, k1)

            outv = out[0].rearrange("(b p) d -> p b d", p=P)
            for half in range(2):
                sp.wait_ge(out_copied, 4 * (half + 1))
                sp.dma_start(outv[:, :, half * S:(half + 1) * S],
                             OUT_T[:, :, half * S:(half + 1) * S]).then_inc(out_stored, 16)
            sp.wait_ge(out_stored, 32)

        @block.tensor
        def _(pe):
            pe.sem_inc(blk_done, 2)
            pe.sem_inc(mixw_trans, 1)

            def products(out_ap, slot, cols, xh, xl, kw, kx, first, last):
                wh, wl = WH[:, slot, kw, cols], WL[:, slot, kw, cols]
                nc.tensor.matmul(out_ap, wh, xh[:, kx, :], start=first, stop=False)
                nc.tensor.matmul(out_ap, wh, xl[:, kx, :], start=False, stop=False)
                return nc.tensor.matmul(out_ap, wl, xh[:, kx, :], start=False, stop=last)

            def half(j):
                return slice(j * P, (j + 1) * P)

            def block_ready(n, slot, use, l):
                pe.wait_ge(w_lo, BLOCKS * l + n + 3)
                pe.wait_ge(bank_free[slot], USES * l + use + 1)

            def weight_block(slot, xh, xl, after=None):
                for k in range(DT):
                    for j in range(2):
                        ins = products(PS[:, 2 * slot + j, :], slot, half(j), xh, xl, k, k, k == 0, k == DT - 1)
                    if k == DT - 1:
                        ins.then_inc(blk_done, 1)
                    if after:
                        after(k)

            def columns(bank, col, sums, n, times):
                pe.wait_ge(mod_ready, times)
                for a in range(n):
                    ins = nc.tensor.matmul(PS[:, bank, col + a:col + a + 1], sums[:, a, :], ONES[:, 0:1],
                                           start=True, stop=True)
                ins.then_inc(ada_cols, 1)

            def statistics(nn):
                pe.wait_ge(sq_added, DT * (nn + 1))
                for b in range(NB):
                    ins = nc.tensor.matmul(PS[:, 4, b:b + 1], ACC[:, b * P:(b + 1) * P], ONES[:, 0:1],
                                           start=True, stop=True)
                ins.then_inc(stat_ready, 1)

            def spread(nn):
                pe.wait_ge(rms_diag, nn + 1)
                nc.tensor.matmul(PS[:, 5, :], ONES[:], DIAG[:].rearrange("p b t -> p (b t)"),
                                 start=True, stop=True).then_inc(rms_wide, 1)

            pe.wait_ge(const_in, 16)
            pe.wait_ge(rows_in, 16 * (7 * DEPTH + 2))
            pe.wait_ge(ones_set, 2)
            for n in range(4):
                ins = nc.tensor.transpose(PS[:, 5, n * VROWS:(n + 1) * VROWS], VR[:, n, :], IDENT[0:VROWS, 0:VROWS])
            ins.then_inc(vec_trans, 1)
            pe.wait_ge(x_in, 16)
            for k in range(DT):
                if k >= 4:
                    pe.wait_ge(x_ready, k - 3)
                for b in range(NB):
                    ins = nc.tensor.transpose(PS[:, k % 4, b * P:(b + 1) * P], XT[:, b, k * P:(k + 1) * P], IDENT)
                ins.then_inc(x_trans, 1)
            pe.wait_ge(cact_ready, 1)

            def first_columns(n):
                if n in PE0:
                    pe.wait_ge(ada0_in[n], 16)
                elif n in POOL0:
                    pe.wait_ge(ada0_pool, POOL0.index(n) + 1)
                else:
                    pe.wait_ge(ada0_sum, SUMS0.index(n) + 1)
                for j in range(2):
                    dst = PS[:, 7, 2 * n + j:2 * n + j + 1]
                    if n in PE0:
                        for k in range(DT):
                            ins = nc.tensor.matmul(dst, ADA0[:, n, k, half(j)], CACT[:, k:k + 1],
                                                   start=k == 0, stop=k == DT - 1)
                    else:
                        ins = nc.tensor.matmul(dst, ADA_ACC0[:, n, half(j)], ONES[:, 0:1], start=True, stop=True)
                return ins

            first_columns(2)
            first_columns(0)
            first_columns(1)
            pe.wait_ge(vec_ready, 1)
            statistics(0)
            first_columns(3)
            spread(0)
            for n in (5, 6, 4):
                first_columns(n)
            first_columns(7).then_inc(ada_cols, 1)
            pe.wait_ge(x_ready, DT)
            pe.wait_ge(vec_ready, 1)

            with pe.Fori(0, DEPTH) as l:
                block_ready(B_K, 0, 0, l)
                block_ready(B_V, 1, 0, l)
                for k in range(DT):
                    pe.wait_ge(h_lo, 2 * DT * l + k + 1)
                    for s in range(2):
                        ins = products(PS[:, 2 * s, :], s, half(0), HH, HL, k, k, k == 0, k == DT - 1)
                        if k == DT - 1:
                            ins.then_inc(blk_done, 1)
                pe.wait_ge(bank_free[1], USES * l + 2)
                for b in range(NB):
                    ins = nc.tensor.transpose(PS[:, 4, b * P:(b + 1) * P], VRAW[:, b * P:(b + 1) * P], IDENT)
                ins.then_inc(v_trans, 1)
                with pe.Fori(0, 2) as i:
                    for s in range(2):
                        block_ready(B_ZV + i * 2 + s, s, U_ZV + i, l)
                        for k in range(DT):
                            for b in range(NB):
                                xh, xl = HH[:, k, b * P:(b + 1) * P], HL[:, k, b * P:(b + 1) * P]
                                dst = PS[:, 2 * s + b // 2, (b % 2) * BC:(b % 2 + 1) * BC]
                                first = k == 0 and b % 2 == 0
                                last = k == DT - 1
                                nc.tensor.matmul(dst, xh, WH[:, s, k, :], start=first, stop=False, skip_group_check=True)
                                nc.tensor.matmul(dst, xh, WL[:, s, k, :], start=False, stop=False, skip_group_check=True)
                                ins = nc.tensor.matmul(dst, xl, WH[:, s, k, :], start=False, stop=last,
                                                       skip_group_check=True)
                        ins.then_inc(blk_done, 1)
                with pe.Fori(0, NQ) as i:
                    def mix_weights():
                        pe.wait_ge(mixw_causal, NQ * l + i + 1)
                        pe.wait_ge(mod_ready, MOD_SUMS * l + i + 1)
                        for g in range(2):
                            ins = nc.tensor.transpose(PS[:, 6, g * P:(g + 1) * P], WRAW[:, g, :], IDENT)
                        ins.then_inc(mixw_trans, 1)

                    def mix_sums():
                        pe.wait_ge(mixw_ready, NQ * l + i + 1)
                        nc.tensor.matmul(PS[:, 6, 0:2 * P], ONES[:], WT[:].rearrange("p g t -> p (g t)"),
                                         start=True, stop=True).then_inc(rowsum_ready, 1)

                    def between_q(k):
                        if k == 3:
                            mix_weights()
                        if k == 7:
                            mix_sums()

                    block_ready(B_Q + i * 4, 0, U_Q + i * 2, l)
                    weight_block(0, HH, HL, between_q)
                    units = NB * DT * l + NB * 2 * i

                    def scores(u):
                        t, b = u // NB, u % NB
                        if u == 0 or u == NB:
                            pe.wait_ge(rope_out, (DT + 1) * l + 2 * i + t + 2)
                        if u < 2:
                            pe.wait_ge(y_raw, 2 * (NQ * l + i) + 1)
                        else:
                            pe.wait_ge(s_used, units + u - 1)
                        keys = slice(max(0, b - 1) * P, (b + 1) * P)
                        width = keys.stop - keys.start
                        dst = PS[:, 4 + u % 2, :].rearrange("p (h k) -> p h k", h=2)[:, :, 0:width]
                        ins = nc.tensor.matmul(dst, QF[:, t, b * P:(b + 1) * P], KP[:, :, keys], start=True, stop=True)
                        ins.then_inc(s_ready, 1)

                    def transposes(u):
                        b = u % NB
                        pe.wait_ge(pn_ready, units + u + 1)
                        if u == 0:
                            pe.wait_ge(mixb_ready, NQ * l + i + 1)
                        else:
                            pe.wait_ge(pt_lo, units + u)
                        for kb in range(0 if b else 1, 2):
                            for h in range(KV_HEADS):
                                ins = nc.tensor.transpose(PS[:, 6, (2 * kb + h) * P:(2 * kb + h + 1) * P],
                                                          SM[u % 2][:, h, kb * P:(kb + 1) * P], IDENT)
                        ins.then_inc(pt_ready, 1)

                    def outputs(u):
                        b = u % NB
                        pe.wait_ge(pt_lo, units + u + 1)
                        if u % 2 == 0:
                            pe.wait_ge(ya_out, 2 * DT * l + 4 * i + u // 2 + 1)
                        if u == 0:
                            pe.wait_ge(v_lo, l + 1)
                        dst = PS[:, 7, (u % 2) * 2 * P:(u % 2 + 1) * 2 * P]
                        kbs = range(0 if b else 1, 2)
                        for kb in kbs:
                            vb = b - 1 + kb
                            for a, (vv, pp) in enumerate(((VH, PTH), (VH, PTL), (VL, PTH))):
                                ins = nc.tensor.matmul(dst, vv[:, vb, :], pp[:, kb].rearrange("p h q -> p (h q)"),
                                                       start=u % 2 == 0 and kb == kbs[0] and a == 0,
                                                       stop=kb == 1 and a == 2, skip_group_check=True)
                        ins.then_inc(o_ready, 1)

                    def mix(g):
                        pe.wait_ge(s_used, units + 7 + g)
                        if g == 0:
                            pe.wait_ge(vn_ready, NQ * l + i + 1)
                        for b in range(NB):
                            ins = nc.tensor.matmul(PS[:, 4 + g, b * P:(b + 1) * P], VN[:, b, g * P:(g + 1) * P],
                                                   WT[:, g, :], start=b == 0, stop=True, skip_group_check=True)
                        ins.then_inc(mixed, 1)

                    def attention_step(w):
                        if w < 8:
                            scores(w)
                        if 0 <= w - 3 < 8:
                            outputs(w - 3)
                        if 0 <= w - 2 < 8:
                            transposes(w - 2)
                        if w >= 9:
                            mix(w - 9)
                        if w == 10:
                            pe.wait_ge(ada_used, ADA_HALVES * l + 8 * i + 8 + 2)
                            columns(6, 0, ADA_ACCA, 4, MOD_SUMS * l + i + 1)

                    def between(k):
                        if k >= 3 and k % 2:
                            attention_step((k - 3) // 2)

                    block_ready(B_Q + i * 4 + 1, 1, U_Q + i * 2, l)
                    weight_block(1, HH, HL, between)
                    block_ready(B_Q + i * 4 + 2, 0, U_Q + i * 2 + 1, l)
                    weight_block(0, HH, HL, lambda k: between(DT + k))
                    block_ready(B_Q + i * 4 + 3, 1, U_Q + i * 2 + 1, l)
                    weight_block(1, HH, HL, lambda k: between(2 * DT + k))

                def merge_iteration(j, before):
                    block_ready(B_M + j * 2, 0, U_M + j, l)
                    before(0)
                    weight_block(0, YSH, YSL, lambda k: before(k + 1) if k + 1 < DT else None)
                    block_ready(B_M + j * 2 + 1, 1, U_M + j, l)
                    before(DT)
                    weight_block(1, YAH, YAL, lambda k: before(DT + k + 1) if k + 1 < DT else None)

                merge_iteration(0, lambda tile: pe.wait_ge(y_lo, 2 * DT * l + tile + 1))
                with pe.Fori(1, NQ) as j:
                    merge_iteration(j, lambda tile: None)

                for b in range(4):
                    block_ready(B_O + b, b % 2, U_O + b // 2, l)
                    if b == 0:
                        pe.wait_ge(m_lo, NQ * l + NQ - 1)
                        weight_block(0, MH, ML, lambda k: pe.wait_ge(m_lo, NQ * l + NQ) if k == DT - 3 else None)
                    else:
                        weight_block(b % 2, MH, ML)
                pe.wait_ge(ada_used, ADA_HALVES * l + 2 * (M_F - M_A) + 2)
                columns(7, 0, ADA_ACCM, DT, MOD_SUMS * l + NQ + 1)

                statistics(2 * l + 1)
                spread(2 * l + 1)
                block_ready(B_F, 0, U_F, l)

                def ffn_iteration(j, normed):
                    if normed is None:
                        block_ready(B_F + j * 2, 0, U_F + j, l)
                    weight_block(0, HH, HL, normed)
                    block_ready(B_F + j * 2 + 1, 1, U_F + j, l)
                    weight_block(1, HH, HL)

                def follow(a):
                    if a + 1 < DT:
                        pe.wait_ge(h_lo, 2 * DT * l + DT + a + 2)

                pe.wait_ge(h_lo, 2 * DT * l + DT + 1)
                ffn_iteration(0, follow)
                with pe.Fori(1, NF) as j:
                    ffn_iteration(j, None)
                pe.wait_ge(ada_used, ADA_HALVES * l + 2 * (M_D - M_A) + 2)
                columns(7, 0, ADA_ACCF, DT, MOD_SUMS * l + NQ + 2)

                with pe.Fori(0, 2) as i:
                    for s in range(2):
                        for n, (k0, k1) in enumerate(SEGS):
                            pe.wait_ge(w_lo, BLOCKS * l + B_D + i * 8 + s * 4 + n + 3)
                            pe.wait_ge(f_lo, NF * l + (k1 + 1) // 2 + 1)
                            if n == 0:
                                pe.wait_ge(bank_free[s], USES * l + U_D + i + 1)
                            for a in range(k1 - k0):
                                for j in range(2):
                                    ins = products(PS[:, 2 * s + j, :], n % 2, half(j), FH, FL, a, k0 + a,
                                                   n == 0 and a == 0, n == 3 and a == k1 - k0 - 1)
                            ins.then_inc(blk_done, 1)

                pe.wait_ge(ada_used, ADA_HALVES * (l + 1) + 2)
                columns(7, 0, ADA_ACCD, 2 * DT, MOD_SUMS * l + NQ + 3)
                statistics(2 * l + 2)
                spread(2 * l + 2)

            for k in range(DT):
                pe.wait_ge(fin_tile, k + 1)
                if k >= 4:
                    pe.wait_ge(out_copied, k - 3)
                for b in range(NB):
                    ins = nc.tensor.transpose(PS[:, k % 4, b * P:(b + 1) * P],
                                              FIN[k % 2][:, k // 2, b * P:(b + 1) * P], IDENT)
                ins.then_inc(out_trans, 1)

        @block.scalar
        def _(act):
            act.sem_inc(w_hi, 2)
            act.sem_inc(ya_out, 1)
            A = nc.scalar.activation

            def hi(n0, slot, l, i=0, per=0, kts=DT, width=BC):
                act.wait_ge(w_loaded[slot], W_INC * ((BLOCKS // 2) * l + n0 // 2 + i * (per // 2) + 1))
                act.wait_ge(blk_done, BLOCKS * l + n0 + i * per + 1)
                A(WH[:, slot, 0:kts, 0:width], WS[:, slot, 0:kts, 0:width], ACT.Copy).then_inc(w_hi, 1)

            def ada_load(l, n0, number, layer, unit):
                half = number % 2
                act.wait_ge(ada_used, ADA_HALVES * l + n0 + number + 1)
                act.dma_start(ADA[:, half:half + 1], ada_v[:, ds(layer, 1), 4 * half:4 * half + 4, ds(unit * P, P)]
                              ).then_inc(ada_loaded[half], 16)

            def rms_root_of(nn):
                act.wait_ge(stat_ready, nn + 1)
                A(RMS[:], PS[:, 4, 0:NB], ACT.Sqrt, bias=EPSC[:, 0:1], scale=1.0 / D).then_inc(rms_root, 1)

            def shifted(nn):
                for k in range(DT):
                    act.wait_ge(h_pre, DT * nn + k + 1)
                    A(HH[:, k, :], NT[k % 2][:], ACT.Identity, bias=SHC[:, k:k + 1]).then_inc(h_hi, 1)

            act.dma_start(VR[V_EXTRA:VROWS, 2, :], c[0].rearrange("(r p) -> r p", p=P)).then_inc(rows_in, 16)
            load_rows(act, 0)
            act.dma_start(VR[V_EXTRA:VROWS, 0, :], final_norm_w.rearrange("(r p) -> r p", p=P)).then_inc(rows_in, 16)
            act.wait_ge(ones_set, 2)
            act.wait_ge(vec_trans, 1)
            A(VEC[:].rearrange("p l t r -> p (l t r)"), PS[:, 5, 0:4 * VROWS], ACT.Copy).then_inc(vec_ready, 1)
            act.wait_ge(vec_ready, 1)
            A(CACT[:], VEC[:, 1, 0, V_EXTRA:V_EXTRA + DT], ACT.Silu).then_inc(cact_ready, 1)
            for k in range(DT):
                act.wait_ge(x_trans, k + 1)
                A(X[:, k, :], PS[:, k % 4, :], ACT.Copy).then_inc(x_ready, 1)
                act.wait_ge(x_ready, k + 1)
                if k >= 2:
                    act.wait_ge(sq_added, k - 1)
                A(SQ0[k % 2][:], X[:, k, :], ACT.Square).then_inc(sq_ready, 1)
            act.wait_ge(angle_ready, 1)
            A(SIN[:], SIN[:], ACT.Sin).then_inc(sine_ready, 1)
            A(COS[:], COS[:], ACT.Sin).then_inc(sine_ready, 1)
            rms_root_of(0)

            with act.Fori(0, DEPTH) as l:
                hi(B_K, 0, l, width=P)
                hi(B_V, 1, l, width=P)
                shifted(2 * l)
                for a in range(2):
                    ada_load(l, 0, a, l, M_A)
                hi(B_ZV, 0, l)
                act.wait_ge(blk_done, BLOCKS * l + B_V + 3)
                A(VRAW[:], PS[:, 2, :], ACT.Copy).then_inc(bank_free[1], 1)
                hi(B_ZV + 1, 1, l)
                act.wait_ge(v_trans, l + 1)
                A(VH[:].rearrange("p b d -> p (b d)"), PS[:, 4, :], ACT.Copy).then_inc(v_hi, 1)
                for b in range(4):
                    act.wait_ge(blk_done, BLOCKS * l + B_ZV + b + 3)
                    A(VT[:, :, b * BC:(b + 1) * BC], bank_pair(b % 2).rearrange("p a (c n) -> p (a c) n", c=2),
                      ACT.Gelu).then_inc(bank_free[b % 2], 1)
                    if b < 3:
                        hi(B_ZV + 2 + b, b % 2, l)
                act.wait_ge(ln_var, l + 1)
                A(SD[:], MV[:, :, 1], ACT.Sqrt, bias=EPSC[:, 0:1]).then_inc(ln_root, 1)

                with act.Fori(0, NQ) as i:
                    hi(B_Q + 1, 1, l, i, 4)
                    for a in (2, 3):
                        ada_load(l, 8 * i, a, l, M_A + 4 * i + a // 2)
                    hi(B_Q + 2, 0, l, i, 4)
                    units = NB * DT * l + NB * 2 * i

                    def exponentials(u):
                        b = u % NB
                        first = 0 if b else P
                        act.wait_ge(nm_ready, units + u + 1)
                        for h in range(KV_HEADS):
                            cols = SM[u % 2][:, h, first:2 * P + 1]
                            ins = A(cols, cols, ACT.Exp, bias=NM[:, u % 2, h:h + 1], accum_out=DEN[:, u % 2, h:h + 1])
                        ins.then_inc(p_ready, 1)

                    def prob_hi(u):
                        first = 0 if u % NB else 1
                        act.wait_ge(pt_ready, units + u + 1)
                        A(PTH[:, first:2].rearrange("p k h q -> p (k h q)"), PS[:, 6, first * 2 * P:],
                          ACT.Copy).then_inc(pt_hi, 1)

                    def attn_out(u):
                        act.wait_ge(o_ready, units + u + 1)
                        alone(act)
                        t, b = u // NB, u % NB - 1
                        src = PS[:, 7, :].rearrange("p (a h q) -> p a h q", a=2, h=2)
                        for h in range(KV_HEADS):
                            rows = slice(h * HD, (h + 1) * HD)
                            dst = YAF[rows, ds(2 * i + t, 1), b * P:(b + 2) * P].rearrange("p o (a q) -> p (o a) q", a=2)
                            ins = A(dst, src[rows, :, h, :], ACT.Copy)
                        ins.then_inc(ya_out, 1)

                    def evacuate(step, dst, func, scale=1.0):
                        act.wait_ge(blk_done, BLOCKS * l + B_Q + i * 4 + step + 3)
                        alone(act)
                        A(dst[:, ds(2 * i, 2), :], bank_pair(step % 2), func, scale=scale).then_inc(bank_free[step % 2], 1)

                    for w in range(11):
                        if w in ADA_LOADS:
                            a = ADA_LOADS[w]
                            ada_load(l, 8 * i, a, l, M_A + 4 * i + a // 2)
                        if 0 <= w - 2 < 8:
                            prob_hi(w - 2)
                        if w < 8:
                            exponentials(w)
                        if w == 10:
                            evacuate(3, YSF, ACT.Gelu)
                        if w - 3 >= 0 and (w - 3) % 2:
                            attn_out(w - 3)
                        if w == 3:
                            evacuate(1, GA, ACT.Tanh, 0.5)
                        if w == 4:
                            hi(B_Q + 3, 1, l, i, 4)
                        if w == 7:
                            evacuate(2, GB, ACT.Tanh, 0.5)
                        if w == 8:
                            hi(B_Q + 4, 0, l, i, 4)

                act.wait_ge(blk_done, BLOCKS * l + B_M + 2)
                for k in range(DT):
                    act.wait_ge(y_raw, DT * l + k + 2)
                    A(YSH[:, k, :], YSF[:, k, :], ACT.Copy).then_inc(y_hi, 1)
                    if k == 1:
                        hi(B_M + 1, 1, l)
                act.wait_ge(ya_out, 2 * DT * (l + 1) + 1)
                for k in range(DT):
                    A(YAH[:, k, :], YAF[:, k, :], ACT.Copy).then_inc(y_hi, 1)

                with act.Fori(0, NQ) as j:
                    n0 = 2 * (M_M - M_A)
                    hi(B_M + 2, 0, l, j, 2)
                    for a in (2, 3):
                        ada_load(l, n0 + 4 * j, a, l, M_M + 2 * j + 1)
                    hi(B_M + 3, 1, l, j, 2)
                    for a in (4, 5):
                        ada_load(l, n0 + 4 * j, a, l, M_M + 2 * j + 2)
                    act.wait_ge(m_sum, NQ * l + j + 1)
                    alone(act)
                    A(MH[:, ds(2 * j, 2), :], GA[:, ds(2 * j, 2), :], ACT.Copy, scale=0.5).then_inc(m_hi, 1)

                def residual_squares(tile, block, s, use):
                    for a in range(2):
                        if a == 0:
                            act.wait_ge(x_ready, DT + DT * l + block + 1)
                        else:
                            act.wait_ge(bank_free[s], USES * l + use + 2)
                        act.wait_ge(sq_added, DT + 2 * DT * l + 2 * block + a - 1)
                        alone(act)
                        A(SQ[a][:], X[:, ds(tile + a, 1), :].rearrange("p o s -> p (o s)"),
                          ACT.Square).then_inc(sq_ready, 1)

                for b in range(4):
                    residual_squares(2 * b, b, b % 2, U_O + b // 2)
                    if b < 3:
                        hi(B_O + 2 + b, b % 2, l)
                rms_root_of(2 * l + 1)
                hi(B_F + 1, 1, l)
                shifted(2 * l + 1)

                def ffn_iteration(j):
                    act.wait_ge(f_lo, NF * l + j + 1)
                    act.wait_ge(blk_done, BLOCKS * l + B_F + j * 2 + 3)
                    for a in range(2):
                        alone(act)
                        A(CONVT[:, a:a + 1, :], PS[:, a:a + 1, :], ACT.Identity,
                          bias=VEC[:, ds(l, 1), 1, ds(CONV * FT + 2 * j + a, 1)].rearrange("p o r -> p (o r)"),
                          scale=VEC[:, ds(l, 1), 1, ds((CONV - 1) * FT + 2 * j + a, 1)].rearrange("p o r -> p (o r)")
                          ).then_inc(conv_pre, 1)
                    hi(B_F + 2, 0, l, j, 2)
                    act.wait_ge(bank_free[0], USES * l + U_F + j + 2)
                    A(CONVT[:], CONVT[:], ACT.Silu).then_inc(silu_done, 1)
                    act.wait_ge(bank_free[1], USES * l + U_F + j + 2)
                    alone(act)
                    A(FH[:, ds(2 * j, 2), :], CONVT[:], ACT.Copy).then_inc(f_hi, 1)
                    hi(B_F + 3, 1, l, j, 2)

                with act.Fori(0, DT - 1) as j:
                    ffn_iteration(j)
                    for a in (2, 3):
                        ada_load(l, 2 * (M_F - M_A) + 2 * j, a, l, M_F + j + 1)
                with act.Fori(DT - 1, NF) as j:
                    ffn_iteration(j)

                other = (DEPTH - 1) - l
                n0 = 2 * (M_D - M_A)
                ada_load(l, n0, 0, other, 0)
                ada_load(l, n0, 1, other, 0)
                for b in range(16):
                    if b + 2 < 16:
                        k0, k1 = SEGS[(b + 2) % 4]
                        hi(B_D + b + 2, b % 2, l, kts=k1 - k0)
                    if b + 1 < 16:
                        ada_load(l, n0, 2 * b + 2, other, b + 1)
                        ada_load(l, n0, 2 * b + 3, other, b + 1)
                    if b % 4 == 3:
                        g = b // 4
                        residual_squares(2 * g, NQ + g, g % 2, U_D + g // 2)
                rms_root_of(2 * l + 2)

            for k in range(DT):
                act.wait_ge(out_trans, k + 1)
                A(OUT_T[:, :, k * P:(k + 1) * P], PS[:, k % 4, :].rearrange("p (b q) -> p b q", b=NB),
                  ACT.Copy).then_inc(out_copied, 1)

        @block.vector
        def _(dve):
            v = nc.vector
            dve.sem_inc(w_lo, 2)
            for s in range(2):
                dve.sem_inc(bank_free[s], 1)
            dve.sem_inc(y_raw, 1)
            dve.sem_inc(ada_used, 2)
            chain = Chain(dve, dve_chain)
            link = chain.link

            def lo(n, slot, l, kts=DT, width=BC):
                dve.wait_ge(w_hi, BLOCKS * l + n + 3)
                v.tensor_tensor(WL[:, slot, 0:kts, 0:width], WS[:, slot, 0:kts, 0:width],
                                WH[:, slot, 0:kts, 0:width], ALU.subtract).then_inc(w_lo, 1)

            def inverse_rms(nn):
                dve.wait_ge(rms_root, nn + 1)
                link(v.reciprocal(RMS[:], RMS[:]))
                v.tensor_tensor(DIAG[:], IDENT.rearrange("p (o t) -> p o t", o=1).to_broadcast([P, NB, P]),
                                RMS[:].rearrange("p (b o) -> p b o", o=1).to_broadcast([P, NB, P]),
                                ALU.mult).then_inc(rms_diag, 1)

            def norm(nn, weight, shift, scale, between=None):
                v.tensor_copy(SHC[:], shift)
                link(v.scalar_tensor_tensor(WSC[:], scale, 1.0, weight, ALU.add, ALU.mult))
                dve.wait_ge(rms_wide, nn + 1)

                def pre(k):
                    v.scalar_tensor_tensor(NT[k % 2][:], X[:, k, :], WSC[:, k:k + 1], PS[:, 5, :], ALU.mult,
                                           ALU.mult).then_inc(h_pre, 1)

                pre(0)
                pre(1)
                if between:
                    between()
                for k in range(DT):
                    dve.wait_ge(h_hi, DT * nn + k + 1)
                    v.scalar_tensor_tensor(HL[:, k, :], NT[k % 2][:], SHC[:, k:k + 1], HH[:, k, :], ALU.add,
                                           ALU.subtract).then_inc(h_lo, 1)
                    if k + 2 < DT:
                        dve.wait_ge(h_lo, DT * nn + k + 1)
                        pre(k + 2)

            def rotate(src, dst):
                alone(dve)
                half = ROT // 2
                v.stream_shuffle(ROTT[:], src, [(p + half) % ROT if p < ROT else p for p in range(32)])
                return v.tensor_tensor(dst, src, COS[:], ALU.mult)

            v.memset(EPSC[:], EPS).then_inc(ones_set, 1)
            dve.wait_ge(pos_in, 16)
            link(v.tensor_copy(T2[:], POS[:]))
            dve.wait_ge(const_in, 16)
            link(v.tensor_scalar(T1[:], T2[:], CST[:, C_FREQ:C_FREQ + 1], None, ALU.mult))
            for quarter, dst in ((0.0, SIN), (0.25, COS)):
                link(v.tensor_scalar(T2[:], T1[:], 1.0 / TWO_PI, quarter, ALU.mult, ALU.add))
                link(v.tensor_scalar(T3[:], T2[:], MAGIC, None, ALU.add))
                link(v.tensor_scalar(T2[:], T3[:], MAGIC, None, ALU.subtract))
                link(v.scalar_tensor_tensor(dst[:], T2[:], -TP1, T1[:], ALU.mult, ALU.add))
                link(v.scalar_tensor_tensor(dst[:], T2[:], -TP2, dst[:], ALU.mult, ALU.add))
                link(v.scalar_tensor_tensor(dst[:], T2[:], -TP3, dst[:], ALU.mult, ALU.add))
                if quarter:
                    link(v.tensor_scalar(dst[:], dst[:], math.pi / 2, None, ALU.add))
                link(v.tensor_scalar(dst[:], dst[:], PI_IN, -PI_IN, ALU.min, ALU.max))
            v.memset(T3[:], 0.0).then_inc(angle_ready, 1)
            dve.wait_ge(cact_ready, 1)
            for n in SUMS0:
                dve.wait_ge(ada0_in[n], 16)
                acc = ADA_ACC0[:, n, :]
                link(v.tensor_scalar(acc, ADA0[:, n, 0, :], CACT[:, 0:1], None, ALU.mult))
                for k in range(1, DT):
                    ins = v.scalar_tensor_tensor(acc, ADA0[:, n, k, :], CACT[:, k:k + 1], acc, ALU.mult, ALU.add)
                    if k < DT - 1:
                        link(ins)
                ins.then_inc(ada0_sum, 1)
                if n == 3:
                    inverse_rms(0)
            dve.wait_ge(sine_ready, 2)
            link(v.tensor_scalar(SIN[:], SIN[:], CST[:, C_SIGN:C_SIGN + 1], None, ALU.mult))
            link(v.tensor_scalar(COS[:], COS[:], CST[:, C_ROT:C_ROT + 1], CST[:, C_PASS:C_PASS + 1],
                                 ALU.mult, ALU.add))
            dve.wait_ge(sinks_in, 16)

            with dve.Fori(0, DEPTH) as l:
                outer = chain.enter(l, LAYER_STEPS)
                lo(B_K, 0, l, width=P)

                def mod_cols(m0, r=l):
                    return MOD[:, ds(r, 1), m0:m0 + DT].rearrange("p o m -> p (o m)")

                def vec_cols(c0):
                    return VEC[:, ds(l, 1), 0, c0:c0 + DT].rearrange("p o m -> p (o m)")

                def modulation(bank, m0, n):
                    return v.tensor_tensor(MOD[:, ds(l, 1), ds(m0, n)], PS[:, bank:bank + 1, 0:n],
                                           VEC[:, ds(l, 1), 0, ds(m0, n)], ALU.add)

                dve.wait_ge(ada_cols, MOD_SUMS * l + 1)
                modulation(7, 0, 2 * DT).then_inc(mod_ready, 1)
                dve.wait_ge(mod_ready, MOD_SUMS * l + 1)
                alone(dve)
                norm(2 * l, vec_cols(V_N1), mod_cols(0), mod_cols(DT), lambda: lo(B_V, 1, l, width=P))
                dve.wait_ge(blk_done, BLOCKS * l + B_K + 3)
                rotate(PS[:, 0, :], T3[:]).then_inc(bank_free[0], 1)
                lo(B_ZV, 0, l)
                lo(B_ZV + 1, 1, l)
                dve.wait_ge(v_hi, l + 1)
                v.tensor_tensor(VL[:].rearrange("p b d -> p (b d)"), PS[:, 4, :],
                                VH[:].rearrange("p b d -> p (b d)"), ALU.subtract).then_inc(v_lo, 1)
                for n in range(4):
                    if n < 3:
                        lo(B_ZV + 2 + n, n % 2, l)
                    dve.wait_ge(bank_free[n % 2], USES * l + U_ZV + n // 2 + 2)
                    for b in range(NB):
                        ins = v.bn_stats(BN[:, b, 6 * n:6 * n + 6], VT[:, b, n * BC:(n + 1) * BC])
                link(ins)
                alone(dve)
                for b in range(NB):
                    ins = v.bn_aggr(MV[:, b, :], BN[:, b, :])
                ins.then_inc(ln_var, 1)
                dve.wait_ge(ln_root, l + 1)
                v.reciprocal(RSV[:], SD[:]).then_inc(ln_ready, 1)
                dve.wait_ge(ln_ready, l + 1)
                alone(dve)

                def ada_half(l, n0, number, unit, acc):
                    half = number % 2
                    dve.wait_ge(ada_loaded[half], 16 * ((ADA_HALVES // 2) * l + unit + 1))
                    for k in range(4):
                        src, ck = ADA[:, half:half + 1, k, :], CACT[:, 4 * half + k:4 * half + k + 1]
                        if half == 0 and k == 0:
                            ins = v.tensor_scalar(acc, src, ck, None, ALU.mult)
                        else:
                            ins = v.scalar_tensor_tensor(acc, src, ck, acc, ALU.mult, ALU.add)
                        if k < 3:
                            link(ins)
                    ins.then_inc(ada_used, 1)
                    if half == 0:
                        dve.wait_ge(ada_used, ADA_HALVES * l + n0 + number + 3)

                with dve.Fori(0, NQ) as i:
                    inner = chain.enter(i, ATTN_STEPS)
                    lo(B_Q + 1 + i * 4, 1, l)
                    dve.wait_ge(mixw_trans, NQ * l + i + 2)
                    v.tensor_copy(WT[:].rearrange("p g t -> p (g t)"), PS[:, 6, 0:2 * P]).then_inc(mixw_ready, 1)

                    def ada_sum(a):
                        ada_half(l, 8 * i, a, 4 * i + a // 2, ADA_ACCA[:, a // 2:a // 2 + 1, :])

                    for a in range(2):
                        ada_sum(a)
                    dve.wait_ge(rowsum_ready, NQ * l + i + 1)
                    dve.wait_ge(mixb_loaded, 16 * (NQ * l + i + 1))
                    for g in range(2):
                        lnb = VEC[:, ds(l, 1), 0, ds(V_LNB + 2 * i + g, 1)].rearrange("p o r -> p (o r)")
                        ins = v.scalar_tensor_tensor(RB[:, g, :], PS[:, 6, g * P:(g + 1) * P], lnb,
                                                     RB[:, g, :], ALU.mult, ALU.add)
                    ins.then_inc(mixb_ready, 1)
                    dve.wait_ge(blk_done, BLOCKS * l + B_Q + i * 4 + 3)
                    for t in range(2):
                        dve.wait_ge(rope_out, (DT + 1) * l + 2 * i + t + 1)
                        ins = rotate(PS[:, t, :], QF[:, t, :])
                        ins.then_inc(rope_cos if t == 0 else bank_free[0], 1)
                    link(v.tensor_copy(SINKC[:], SINK[:, ds(l, 1), :, ds(2 * i, 2)].rearrange("p o h t -> p (o h) t")))
                    units = NB * DT * l + NB * 2 * i

                    def mask_and_max(u):
                        t, b = u // NB, u % NB
                        first = 0 if b else P
                        dve.wait_ge(s_ready, units + u + 1)
                        if u >= 2:
                            dve.wait_ge(pt_ready, units + u - 1)
                        v.tensor_copy(SM[u % 2][:, :, 2 * P:2 * P + 1], SINKC[:, :, t:t + 1])
                        for h in range(KV_HEADS):
                            ins = v.tensor_tensor_reduce(
                                out=SM[u % 2][:, h, first:2 * P],
                                in0=PS[:, 4 + u % 2, h * 2 * P:h * 2 * P + 2 * P - first],
                                in1=CST[:, C_MASK + first:C_MASK + 2 * P], scale=HD ** -0.5,
                                scalar=SINKC[:, h, t:t + 1],
                                op0=ALU.add, op1=ALU.max, accum_out=MX[:, u % 2, h:h + 1])
                        ins.then_inc(s_used, 1)
                        dve.wait_ge(s_used, units + u + 1)
                        v.tensor_scalar(NM[:, u % 2, :], MX[:, u % 2, :], -1.0, None, ALU.mult).then_inc(nm_ready, 1)

                    def inverse(u):
                        dve.wait_ge(p_ready, units + u + 1)
                        v.reciprocal(RDEN[:, u % 2, :], DEN[:, u % 2, :]).then_inc(rden_ready, 1)

                    def prob_lo(u):
                        first = 0 if u % NB else 1
                        dve.wait_ge(pt_hi, units + u + 1)
                        v.tensor_tensor(PTL[:, first:2].rearrange("p k h q -> p (k h q)"), PS[:, 6, first * 2 * P:],
                                        PTH[:, first:2].rearrange("p k h q -> p (k h q)"),
                                        ALU.subtract).then_inc(pt_lo, 1)

                    for w in range(11):
                        if w < 8:
                            mask_and_max(w)
                        if 0 <= w - 2 < 8:
                            prob_lo(w - 2)
                        if w < 8:
                            if w in ADA_SUMS:
                                ada_sum(ADA_SUMS[w])
                            inverse(w)
                        if 5 <= w < 5 + NB:
                            b = w - 5
                            ins = v.tensor_scalar(VN[:, b:b + 1, :], VT[:, b:b + 1, ds(BC * i, BC)], MV[:, b, 0:1],
                                                  RSV[:, b:b + 1], ALU.subtract, ALU.mult)
                            if b == NB - 1:
                                ins.then_inc(vn_ready, 1)
                        if w == 0:
                            lo(B_Q + 2 + i * 4, 0, l)
                        if w == 4:
                            lo(B_Q + 3 + i * 4, 1, l)
                        if w == 8:
                            lo(B_Q + 4 + i * 4, 0, l)
                    dve.wait_ge(mixb_ready, NQ * l + i + 1)
                    for g in range(2):
                        lnw = VEC[:, ds(l, 1), 0, ds(V_LNW + 2 * i + g, 1)].rearrange("p o r -> p (o r)")
                        dve.wait_ge(mixed, 2 * (NQ * l + i) + g + 1)
                        m = PS[:, 4 + g, :].rearrange("p (b t) -> p b t", b=NB)
                        link(v.scalar_tensor_tensor(m, m, lnw, RB[:, g:g + 1, :].to_broadcast([P, NB, P]),
                                                    ALU.mult, ALU.add))
                    dve.wait_ge(bank_free[1], USES * l + U_Q + 2 * i + 3)
                    for g in range(2):
                        v.tensor_tensor(YSF[:, ds(2 * i + g, 1), :], PS[:, 4 + g:5 + g, :],
                                        YSF[:, ds(2 * i + g, 1), :], ALU.mult).then_inc(y_raw, 1)
                    dve.wait_ge(ada_cols, MOD_SUMS * l + i + 2)
                    modulation(6, M_A + 4 * i, 4).then_inc(mod_ready, 1)
                    chain.leave(inner, NQ)

                for k in range(DT):
                    dve.wait_ge(y_hi, 2 * DT * l + k + 1)
                    v.tensor_tensor(YSL[:, k, :], YSF[:, k, :], YSH[:, k, :], ALU.subtract).then_inc(y_lo, 1)
                    if k == 1:
                        lo(B_M + 1, 1, l)
                for k in range(DT):
                    dve.wait_ge(y_hi, 2 * DT * l + DT + k + 1)
                    v.tensor_tensor(YAL[:, k, :], YAF[:, k, :], YAH[:, k, :], ALU.subtract).then_inc(y_lo, 1)

                with dve.Fori(0, NQ) as j:
                    inner = chain.enter(j, MERGE_STEPS)

                    def halves(first):
                        for a in (first, first + 1):
                            ada_half(l, 2 * (M_M - M_A) + 4 * j, a, M_M - M_A + 2 * j + a // 2,
                                     ADA_ACCM[:, ds(2 * j + a // 2, 1), :])

                    halves(0)
                    dve.wait_ge(blk_done, BLOCKS * l + B_M + j * 2 + 3)
                    v.scalar_tensor_tensor(GA[:, ds(2 * j, 2), :], GA[:, ds(2 * j, 2), :], 1.0, bank_pair(0),
                                           ALU.add, ALU.mult).then_inc(bank_free[0], 1)
                    lo(B_M + 2 + j * 2, 0, l)
                    halves(2)
                    dve.wait_ge(blk_done, BLOCKS * l + B_M + j * 2 + 1 + 3)
                    v.scalar_tensor_tensor(GB[:, ds(2 * j, 2), :], GB[:, ds(2 * j, 2), :], 1.0, bank_pair(1),
                                           ALU.add, ALU.mult).then_inc(bank_free[1], 1)
                    lo(B_M + 3 + j * 2, 1, l)
                    dve.wait_ge(m_hi, NQ * l + j + 1)
                    v.scalar_tensor_tensor(ML[:, ds(2 * j, 2), :], GA[:, ds(2 * j, 2), :], 0.5,
                                           MH[:, ds(2 * j, 2), :], ALU.mult, ALU.subtract).then_inc(m_lo, 1)
                    chain.leave(inner, NQ)

                def add_residual(slot, tile, gate):
                    for a in range(2):
                        g = MOD[:, ds(l, 1), ds(gate + tile + a, 1)].rearrange("p o m -> p (o m)")
                        xt = X[:, ds(tile + a, 1), :]
                        v.scalar_tensor_tensor(xt, PS[:, 2 * slot + a:2 * slot + a + 1, :], g, xt, ALU.mult,
                                               ALU.add).then_inc(bank_free[slot] if a else x_ready, 1)

                def last_squares(nn):
                    for a in range(2):
                        dve.wait_ge(sq_ready, DT * nn + DT - 1 + a)
                        dve.wait_ge(sq_added, DT * nn + DT - 2 + a)
                        v.tensor_tensor(ACC[:], ACC[:], SQ[a][:], ALU.add).then_inc(sq_added, 1)

                dve.wait_ge(mod_ready, MOD_SUMS * l + NQ + 1)
                for b in range(4):
                    dve.wait_ge(blk_done, BLOCKS * l + B_O + b + 3)
                    add_residual(b % 2, 2 * b, M_A)
                    if b == 3:
                        last_squares(2 * l + 1)
                        dve.wait_ge(ada_cols, MOD_SUMS * l + NQ + 2)
                        modulation(7, M_M, DT).then_inc(mod_ready, 1)
                        dve.wait_ge(mod_ready, MOD_SUMS * l + NQ + 2)
                    else:
                        lo(B_O + 2 + b, b % 2, l)

                inverse_rms(2 * l + 1)
                norm(2 * l + 1, vec_cols(V_N2), mod_cols(3 * DT), mod_cols(4 * DT))

                def ffn_iteration(j, with_ada):
                    for a in range(2):
                        dve.wait_ge(conv_pre, 2 * (NF * l + j) + a + 1)
                        for tap in (1, 0):
                            lag = CONV - 1 - tap
                            wt = VEC[:, ds(l, 1), 1, ds(tap * FT + 2 * j + a, 1)].rearrange("p o r -> p (o r)")
                            dst = CONVT[:, a:a + 1, lag:]
                            ins = v.scalar_tensor_tensor(dst, PS[:, a:a + 1, 0:S - lag], wt, dst, ALU.mult, ALU.add)
                            if not (a == 1 and tap == 0):
                                link(ins)
                    ins.then_inc(bank_free[0], 1)
                    dve.wait_ge(w_lo, BLOCKS * l + B_F + 2 * j + 4)
                    lo(B_F + 2 + j * 2, 0, l)
                    if with_ada:
                        for a in range(2):
                            ada_half(l, 2 * (M_F - M_A) + 2 * j, a, M_F - M_A + j, ADA_ACCF[:, ds(j, 1), :])
                    dve.wait_ge(silu_done, NF * l + j + 1)
                    dve.wait_ge(blk_done, BLOCKS * l + B_F + j * 2 + 1 + 3)
                    v.tensor_tensor(CONVT[:], CONVT[:], bank_pair(1), ALU.mult).then_inc(bank_free[1], 1)
                    lo(B_F + 3 + j * 2, 1, l)

                with dve.Fori(0, DT) as j:
                    inner = chain.enter(j, FFN_STEPS[0])
                    ffn_iteration(j, True)
                    chain.leave(inner, DT)
                with dve.Fori(DT, NF) as j:
                    inner = chain.enter(j - DT, FFN_STEPS[1])
                    ffn_iteration(j, False)
                    chain.leave(inner, NF - DT)
                dve.wait_ge(ada_cols, MOD_SUMS * l + NQ + 3)
                modulation(7, M_F, DT).then_inc(mod_ready, 1)
                dve.wait_ge(mod_ready, MOD_SUMS * l + NQ + 3)

                for b in range(16):
                    for a in range(2):
                        ada_half(l, 2 * (M_D - M_A), 2 * b + a, M_D - M_A + b, ADA_ACCD[:, b:b + 1, :])
                    if b % 4 == 3:
                        dve.wait_ge(blk_done, BLOCKS * l + B_D + b + 3)
                        add_residual((b // 4) % 2, b // 4 * 2, M_F)
                    if b == 15:
                        last_squares(2 * l + 2)
                    if b + 2 < 16:
                        k0, k1 = SEGS[(b + 2) % 4]
                        lo(B_D + b + 2, b % 2, l, kts=k1 - k0)
                inverse_rms(2 * l + 2)
                chain.leave(outer, DEPTH)

            dve.wait_ge(rms_wide, 2 * DEPTH + 1)
            for k in range(DT):
                dst = FIN[k % 2][:, k // 2, :]
                v.scalar_tensor_tensor(dst, X[:, k, :], VEC[:, 0, 0, V_EXTRA + k:V_EXTRA + k + 1], PS[:, 5, :], ALU.mult,
                                       ALU.mult).then_inc(fin_tile, 1)

        @block.gpsimd
        def _(pool):
            g_ = nc.gpsimd
            chain = Chain(pool, pool_chain)
            link = chain.link
            pool.sem_inc(f_lo, 1)
            g_.memset(ONES[:], 1.0).then_inc(ones_set, 1)

            def add_square(nn_count, src):
                pool.wait_ge(sq_ready, nn_count + 1)
                g_.tensor_tensor(ACC[:], ACC[:], src, ALU.add).then_inc(sq_added, 1)
                pool.wait_ge(sq_added, nn_count + 1)

            pool.wait_ge(angle_ready, 1)
            g_.memset(ACC[:], 0.0).then_inc(acc_zero, 1)
            pool.wait_ge(acc_zero, 1)
            for k in range(DT):
                add_square(k, SQ0[k % 2][:])
            pool.wait_ge(x_ready, DT)
            for n in POOL0:
                pool.wait_ge(ada0_in[n], 16)
                products = ADA0[:, n]
                link(g_.tensor_tensor(products, products, CACT[:].rearrange("p (k o) -> p k o", o=1)
                                      .to_broadcast([P, DT, BC]), ALU.mult))
                for m in (DT // 2, DT // 4):
                    link(g_.tensor_tensor(products[:, 0:m], products[:, 0:m], products[:, m:2 * m], ALU.add))
                g_.tensor_tensor(ADA_ACC0[:, n, :], products[:, 0, :], products[:, 1, :],
                                 ALU.add).then_inc(ada0_pool, 1)
            pool.wait_ge(ada0_pool, len(POOL0))

            with pool.Fori(0, DEPTH) as l:
                outer = chain.enter(l, POOL_LAYER_STEPS)

                pool.wait_ge(stat_ready, 2 * l + 1)
                alone(pool)
                link(g_.memset(KP[HD:P, 0, :], 0.0))
                alone(pool)
                link(g_.memset(KP[0:HD, 1, :], 0.0))
                pool.wait_ge(bank_free[0], USES * l + 2)
                link(g_.tensor_tensor(ROTT[:], ROTT[:], SIN[:], ALU.mult))
                for h in range(KV_HEADS):
                    rows = slice(h * HD, (h + 1) * HD)
                    ins = g_.tensor_tensor(KP[rows, h, :], T3[rows, :], ROTT[rows, :], ALU.add)
                ins.then_inc(rope_out, 1)

                def turn(f):
                    link(g_.tensor_tensor(ROTT[:], ROTT[:], SIN[:], ALU.mult))
                    g_.tensor_tensor(f, f, ROTT[:], ALU.add).then_inc(rope_out, 1)

                with pool.Fori(0, NQ) as i:
                    inner = chain.enter(i, 2)
                    pool.wait_ge(rope_out, (DT + 1) * l + 2 * i + 1)
                    pool.wait_ge(mixw_loaded, 16 * (NQ * l + i + 1))
                    alone(pool)
                    g_.affine_select(out=WRAW[:], in_=WRAW[:], compare_op=ALU.is_ge, fill=0.0, base=0,
                                     pattern=[[0, 2], [-1, P]], channel_multiplier=1).then_inc(mixw_causal, 1)
                    pool.wait_ge(rope_cos, NQ * l + i + 1)
                    turn(QF[:, 0, :])
                    pool.wait_ge(bank_free[0], USES * l + U_Q + 2 * i + 2)
                    turn(QF[:, 1, :])
                    units = NB * DT * l + NB * 2 * i
                    for u in range(8):
                        first = 0 if u % NB else P
                        pool.wait_ge(rden_ready, units + u + 1)
                        alone(pool)
                        for h in range(KV_HEADS):
                            cols = SM[u % 2][:, h, first:2 * P]
                            ins = g_.tensor_scalar(cols, cols, RDEN[:, u % 2, h:h + 1], None, ALU.mult)
                        ins.then_inc(pn_ready, 1)
                    chain.leave(inner, NQ)
                with pool.Fori(0, NQ) as j:
                    pool.wait_ge(bank_free[1], USES * l + U_M + j + 2)
                    g_.tensor_tensor(GA[:, ds(2 * j, 2), :], GA[:, ds(2 * j, 2), :], GB[:, ds(2 * j, 2), :],
                                     ALU.add).then_inc(m_sum, 1)

                def sum_squares(nn):
                    pool.wait_ge(stat_ready, nn)
                    alone(pool)
                    link(g_.memset(ACC[:], 0.0))
                    alone(pool)
                    with pool.Fori(0, DT // 2 - 1) as m:
                        for a in range(2):
                            add_square(DT * nn + 2 * m + a, SQ[a][:])

                sum_squares(2 * l + 1)
                pool.wait_ge(w_hi, BLOCKS * l + B_F + 1 + 3)
                g_.tensor_tensor(WL[:, 1], WS[:, 1], WH[:, 1], ALU.subtract).then_inc(w_lo, 1)
                with pool.Fori(0, NF) as j:
                    pool.wait_ge(f_hi, NF * l + j + 1)
                    g_.tensor_tensor(FL[:, ds(2 * j, 2), :], CONVT[:], FH[:, ds(2 * j, 2), :],
                                     ALU.subtract).then_inc(f_lo, 1)
                sum_squares(2 * l + 2)
                chain.leave(outer, DEPTH)


LAYER_STEPS, ATTN_STEPS, MERGE_STEPS, FFN_STEPS, POOL_LAYER_STEPS = 338, 27, 12, (9, 3), 13

_INS = ["x", "c", "positions", "ada_w", "ada_b", "norm1_w", "w_in", "attn_sinks", "sgu_ln_w", "sgu_ln_b", "sgu_w",
        "sgu_b", "proj_a", "proj_b", "w_out", "norm2_w", "ffn_w_gate", "ffn_w_up", "ffn_conv_w", "ffn_conv_b",
        "ffn_w_down", "final_norm_w"]


def kernel(**inputs):
    import concourse.bacc as _bacc
    from concourse.bass_utils import run_bass_kernel_spmd as _run

    nc = _bacc.Bacc("TRN2", target_bir_lowering=False, num_devices=1, dynamic_dma_scratch_size=64)
    arrays, args = {}, []
    for name in _INS:
        a = np.ascontiguousarray(inputs[name])
        arrays[f"in_{name}"] = a
        args.append(nc.dram_tensor(f"in_{name}", a.shape, mybir.dt.from_np(a.dtype), kind="ExternalInput").ap())
    a = shape_constants()
    arrays["shape_constants"] = a
    args.append(nc.dram_tensor("shape_constants", a.shape, F32, kind="ExternalInput").ap())
    args.append(nc.dram_tensor("out", (1, S, D), F32, kind="ExternalOutput").ap())
    trunk_kernel(nc, *args)
    r = _run(nc, [arrays], core_ids=[0])
    return r.results[0]["out"]
```
